# Optimizing a Trainium2 kernel written in Bass

```python
import jax, jax.numpy as jnp
from jax import lax
import numpy as np

D_MODEL = 1024
BATCH = 1
SEQ = 512
DEPTH = 2

D_MIX = D_MODEL
D_RNN = D_MIX // 2
D_RET = D_MIX - D_RNN
N_RNN_BLOCKS = 8
RNN_BLOCK = D_RNN // N_RNN_BLOCKS
CONV_WIDTH = 4
LRU_C = 8.0
N_RET_HEADS = 4
RET_HEAD_DIM = D_RET // N_RET_HEADS
CHUNK = 128
ROPE_BASE = 10000.0
D_FF = 2816
EPS = 1e-6
IN_SPLITS = [D_RNN, D_RNN, D_RET, D_RET, D_RET, D_RET]
D_IN = sum(IN_SPLITS)

kernel_name = 'hymba_rglru_retention_macaron'

def rmsnorm(x, g):
    xf = x.astype(jnp.float32)
    y = xf * lax.rsqrt(jnp.mean(xf * xf, axis=-1, keepdims=True) + EPS)
    return (y * g.astype(jnp.float32)).astype(x.dtype)

def head_rmsnorm(y):
    yf = y.astype(jnp.float32)
    return yf * lax.rsqrt(jnp.mean(yf * yf, axis=-1, keepdims=True) + EPS)

def swiglu(x, w_in, w_out):
    gate, up = jnp.split(x @ w_in, 2, axis=-1)
    return (jax.nn.silu(gate) * up) @ w_out

def causal_dwconv(x, w, b):
    seq = x.shape[1]
    k_taps = w.shape[0]
    xp = jnp.pad(x, ((0, 0), (k_taps - 1, 0), (0, 0)))
    y = xp[:, 0:seq] * w[0]
    for k in range(1, k_taps):
        y = y + xp[:, k:k + seq] * w[k]
    return y + b

def rg_lru(x, gate_a_w, gate_a_b, gate_x_w, gate_x_b, lam):
    bsz, seq, ch = x.shape
    xh = x.reshape(bsz, seq, N_RNN_BLOCKS, RNN_BLOCK)
    r_gate = jax.nn.sigmoid(jnp.einsum('bshi,hij->bshj', xh, gate_a_w).reshape(bsz, seq, ch) + gate_a_b).astype(jnp.float32)
    i_gate = jax.nn.sigmoid(jnp.einsum('bshi,hij->bshj', xh, gate_x_w).reshape(bsz, seq, ch) + gate_x_b).astype(jnp.float32)
    log_a = -LRU_C * r_gate * jax.nn.softplus(-lam.astype(jnp.float32))
    a = jnp.exp(log_a)
    u = jnp.sqrt(-jnp.expm1(2.0 * log_a)) * (i_gate * x.astype(jnp.float32))

    def combine(left, right):
        a1, b1 = left
        a2, b2 = right
        return a1 * a2, a2 * b1 + b2

    _, h = lax.associative_scan(combine, (a, u), axis=1)
    return h.astype(x.dtype)

def rotary(t, positions):
    half = t.shape[-1] // 2
    inv_freq = ROPE_BASE ** (-jnp.arange(half, dtype=jnp.float32) / half)
    ang = positions.astype(jnp.float32)[..., None] * inv_freq
    cos = jnp.cos(ang)[:, :, None, :]
    sin = jnp.sin(ang)[:, :, None, :]
    t1 = t[..., :half].astype(jnp.float32)
    t2 = t[..., half:].astype(jnp.float32)
    return jnp.concatenate([t1 * cos - t2 * sin, t1 * sin + t2 * cos], axis=-1).astype(t.dtype)

def chunkwise_retention(q, k, v, positions):
    bsz, seq, n_heads, dh = q.shape
    n_chunks = seq // CHUNK
    q = rotary(q, positions)
    k = rotary(k, positions) * (dh ** -0.5)
    log_gamma = jnp.log1p(-(2.0 ** (-5.0 - jnp.arange(n_heads, dtype=jnp.float32))))
    idx = jnp.arange(CHUNK, dtype=jnp.float32)
    rel = idx[:, None] - idx[None, :]
    decay = jnp.where(rel >= 0, jnp.exp(jnp.maximum(rel, 0.0)[None] * log_gamma[:, None, None]), 0.0)
    xi = jnp.exp((idx + 1.0)[None, :] * log_gamma[:, None])
    zeta = jnp.exp((CHUNK - 1.0 - idx)[None, :] * log_gamma[:, None])
    chunk_decay = jnp.exp(CHUNK * log_gamma)

    qc = q.reshape(bsz, n_chunks, CHUNK, n_heads, dh)
    kc = k.reshape(bsz, n_chunks, CHUNK, n_heads, dh)
    vc = v.reshape(bsz, n_chunks, CHUNK, n_heads, dh)

    scores = jnp.einsum('bnchd,bnmhd->bnhcm', qc, kc) * decay
    inner = jnp.einsum('bnhcm,bnmhe->bnche', scores, vc)
    kv = jnp.einsum('bnmhd,bnmhe,hm->nbhde', kc, vc, zeta)

    def step(state, kv_i):
        return chunk_decay[None, :, None, None] * state + kv_i, state

    _, prev = lax.scan(step, jnp.zeros(kv.shape[1:], kv.dtype), kv)
    cross = jnp.einsum('bnchd,nbhde->bnche', qc, prev) * xi.T[None, None, :, :, None]
    return (inner + cross).reshape(bsz, seq, n_heads, dh)

def setup_inputs(seed: int = 0) -> dict:
    key = jax.random.key(seed)
    ks = jax.random.split(key, 24)
    f32 = jnp.float32
    L = DEPTH

    def nrm(k, shape, scale):
        return jax.random.normal(k, shape, f32) * scale

    u = jax.random.uniform(ks[12], (L, D_RNN), f32, minval=0.9, maxval=0.999)
    a_base = u ** (1.0 / LRU_C)
    lru_lambda = jnp.log(a_base) - jnp.log1p(-a_base)
    offsets = jax.random.randint(ks[20], (BATCH, 1), 0, 4096, dtype=jnp.int32)
    positions = offsets + jnp.arange(SEQ, dtype=jnp.int32)[None, :]
    return {
        'x': nrm(ks[0], (BATCH, SEQ, D_MODEL), 1.0),
        'positions': positions,
        'norm_ffn1': 1.0 + nrm(ks[1], (L, D_MODEL), 0.02),
        'w_ffn1_in': nrm(ks[2], (L, D_MODEL, 2 * D_FF), D_MODEL ** -0.5),
        'w_ffn1_out': nrm(ks[3], (L, D_FF, D_MODEL), D_FF ** -0.5),
        'norm_mix': 1.0 + nrm(ks[4], (L, D_MODEL), 0.02),
        'w_in': nrm(ks[5], (L, D_MODEL, D_IN), D_MODEL ** -0.5),
        'conv_w': nrm(ks[6], (L, CONV_WIDTH, D_RNN), CONV_WIDTH ** -0.5),
        'conv_b': nrm(ks[7], (L, D_RNN), 0.01),
        'gate_a_w': nrm(ks[8], (L, N_RNN_BLOCKS, RNN_BLOCK, RNN_BLOCK), RNN_BLOCK ** -0.5),
        'gate_a_b': nrm(ks[9], (L, D_RNN), 0.01),
        'gate_x_w': nrm(ks[10], (L, N_RNN_BLOCKS, RNN_BLOCK, RNN_BLOCK), RNN_BLOCK ** -0.5),
        'gate_x_b': nrm(ks[11], (L, D_RNN), 0.01),
        'lru_lambda': lru_lambda,
        'w_out': nrm(ks[13], (L, D_MIX, D_MODEL), D_MIX ** -0.5),
        'norm_ffn2': 1.0 + nrm(ks[14], (L, D_MODEL), 0.02),
        'w_ffn2_in': nrm(ks[15], (L, D_MODEL, 2 * D_FF), D_MODEL ** -0.5),
        'w_ffn2_out': nrm(ks[16], (L, D_FF, D_MODEL), D_FF ** -0.5),
        'norm_final': 1.0 + nrm(ks[17], (D_MODEL,), 0.02),
    }

def reference(x, positions, norm_ffn1, w_ffn1_in, w_ffn1_out, norm_mix, w_in, conv_w, conv_b,
              gate_a_w, gate_a_b, gate_x_w, gate_x_b, lru_lambda, w_out, norm_ffn2,
              w_ffn2_in, w_ffn2_out, norm_final):
    bsz, seq, _ = x.shape
    split_idx = [int(s) for s in np.cumsum(IN_SPLITS)[:-1]]
    for l in range(DEPTH):
        x = x + 0.5 * swiglu(rmsnorm(x, norm_ffn1[l]), w_ffn1_in[l], w_ffn1_out[l])

        h = rmsnorm(x, norm_mix[l])
        proj = h @ w_in[l]
        rnn_x, rnn_gate, q, k, v, g = jnp.split(proj, split_idx, axis=-1)

        rnn_x = causal_dwconv(rnn_x, conv_w[l], conv_b[l])
        rnn_y = rg_lru(rnn_x, gate_a_w[l], gate_a_b[l], gate_x_w[l], gate_x_b[l], lru_lambda[l])
        rnn_y = rnn_y * jax.nn.gelu(rnn_gate)

        heads = (bsz, seq, N_RET_HEADS, RET_HEAD_DIM)
        ret = chunkwise_retention(q.reshape(heads), k.reshape(heads), v.reshape(heads), positions)
        ret_y = head_rmsnorm(ret).reshape(bsz, seq, D_RET).astype(x.dtype) * jax.nn.silu(g)

        x = x + jnp.concatenate([rnn_y, ret_y], axis=-1) @ w_out[l]

        x = x + 0.5 * swiglu(rmsnorm(x, norm_ffn2[l]), w_ffn2_in[l], w_ffn2_out[l])
    return rmsnorm(x, norm_final)


_drawn_inputs = setup_inputs


def setup_inputs(seed=0):
    import zlib

    import numpy as np

    out = dict(_drawn_inputs(seed))
    spreads = {}
    factors = {'norm_ffn1': 3.651,
     'gate_a_b': 64.0,
     'gate_x_b': 64.0,
     'norm_ffn2': 18.48,
     'norm_final': 23.674,
     'norm_mix': 7.62,
     'conv_b': 6.991}
    for name, (base, spread) in spreads.items():
        noise = np.random.default_rng([zlib.crc32(name.encode()), seed]).standard_normal(out[name].shape)
        drawn = base * np.exp(spread * noise) if base else spread * noise
        out[name] = __import__('jax').numpy.asarray(drawn.astype(out[name].dtype))
    for name, factor in factors.items():
        out[name] = (out[name] * factor).astype(out[name].dtype)
    return out
```

```python
from contextlib import ExitStack

import concourse.bass as bass
from concourse import mybir

F32 = mybir.dt.float32
F32R = mybir.dt.float32r
I32 = mybir.dt.int32
ALU = mybir.AluOpType
ACT = mybir.ActivationFunctionType

P = 128
T = 512
D = 1024
DEPTH = 2
FF = 2816
HEADS = 4
DH = 128
LRU_C = 8.0
EPS = 1e-6
KC = D // P
FC = FF // P
TC = T // P
RC = 4

RING = 4
PIECE = KC
DOWN = (6, 6, 5, 5)
assert sum(DOWN) == FC

UP_Q, DOWN_Q, PROJ_Q, MERGE_Q = 2 * FC // RING, KC, 6, KC // RING
FFN_Q, MIX_Q = UP_Q + DOWN_Q, PROJ_Q + MERGE_Q
LAYER_Q = 2 * FFN_Q + MIX_Q
FFN_AT = (0, FFN_Q + MIX_Q)
MIX_AT = FFN_Q
FFN_O, MIX_O = RING * UP_Q + KC, RING * PROJ_Q + KC
LAYER_O = 2 * FFN_O + MIX_O
FFN_O_AT = (0, FFN_O + MIX_O)
MIX_O_AT = FFN_O
NORMS = 3 * DEPTH + 1
NORM_OF_FFN = (0, 2)
NORM_OF_MIX = 1
YS = HEADS + RC

G_AT = 0
CONV_W_AT = G_AT + NORMS * KC
CONV_B_AT = CONV_W_AT + DEPTH * 4 * RC
GATE_A_B_AT = CONV_B_AT + DEPTH * RC
GATE_X_B_AT = GATE_A_B_AT + DEPTH * RC
LAM_AT = GATE_X_B_AT + DEPTH * RC
FREQ_AT = LAM_AT + DEPTH * RC
NPAR = FREQ_AT + 1
TAPS = 4

TWO_PI_UNIT = 10 ** 36
TWO_PI_UNITS = 6283185307179586476925286766559005768
TWO_PI = TWO_PI_UNITS / TWO_PI_UNIT
PI_BELOW = 3.1415925
TURN = 2048.0
ROUND = 1.5 * 2.0 ** 23


def two_pi_parts():
    parts, taken, last = [], 0, 52
    for bits in (8, 19, 30, 41):
        digits = (TWO_PI_UNITS << bits) // TWO_PI_UNIT << (last - bits)
        parts.append((digits - taken) / 2.0 ** last)
        taken = digits
    return parts + [((TWO_PI_UNITS << last) // TWO_PI_UNIT - taken) / 2.0 ** last]


TURN_PARTS = two_pi_parts()
TRIG_STEPS = 20


def build(nc, xT, positions, params, w_up, w_down, w_proj, w_merge, gates, decay, eye, out):
    ctx = ExitStack()
    with ctx:
        def sb(name, shape, dt=F32):
            return ctx.enter_context(nc.sbuf_tensor(name, shape, dt))

        def sem(name):
            return ctx.enter_context(nc.semaphore(name))

        x = sb("x_sb", [P, KC, T])
        xg_hi = sb("xg_hi", [P, KC, T], F32R)
        xg_lo = sb("xg_lo", [P, KC, T], F32R)
        raw = sb("raw", [P, RING, PIECE, P])
        w_hi = sb("w_hi", [P, RING, PIECE, P], F32R)
        w_lo = sb("w_lo", [P, RING, PIECE, P], F32R)
        rms = sb("rms", [P, T])
        square = sb("square", [P, T])
        sumsq = sb("sumsq", [P, T])
        tmp0 = sb("tmp0", [P, T])
        tmp1 = sb("tmp1", [P, T])
        cos = sb("cos", [P, T])
        sin = sb("sin", [P, T])
        angle = sb("angle", [P, T])
        par = sb("par", [P, NPAR])
        ones = sb("ones", [P, P])
        ident = sb("ident", [P, P])
        eps = sb("eps", [P, 1])
        one = sb("one", [P, 1])
        half_pi = sb("half_pi", [P, 1])
        lru_pos = sb("lru_pos", [P, DEPTH * RC])
        lru_neg = sb("lru_neg", [P, DEPTH * RC])
        soft = sb("soft", [P, 4, DEPTH * RC])

        hidden = ExitStack()
        h_hi = hidden.enter_context(nc.sbuf_tensor("h_hi", [P, FC, T], F32R))
        h_lo = hidden.enter_context(nc.sbuf_tensor("h_lo", [P, FC, T], F32R))
        hidden.close()
        y_hi = sb("y_hi", [P, YS, T], F32R)
        y_lo = sb("y_lo", [P, YS, T], F32R)
        dec = sb("dec", [P, HEADS, T])
        gate_w = sb("gate_w", [P, 2, RC, P])
        gate_now = sb("gate_now", [P, 2, P])
        xr = sb("xr", [P, RC, TAPS - 1 + T])
        xc = sb("xc", [P, T])
        r_gate = sb("r_gate", [P, T])
        i_gate = sb("i_gate", [P, T])
        a_dec = sb("a_dec", [P, T])
        a_mult = sb("a_mult", [P, T])
        cos_r = sb("cos_r", [P, T])
        sin_r = sb("sin_r", [P, T])
        q = sb("q", [P, T])
        k = sb("k", [P, T])
        vT = sb("vT", [P, T])
        v_tok = sb("v_tok", [P, TC, P])
        probs = sb("probs", [P, sum(T - j * P for j in range(TC))])
        g_silu = sb("g_silu", [P, T])
        head_rms = sb("head_rms", [P, T])
        yv = sb("yv", [P, T])
        yv2 = sb("yv2", [P, T])
        first_square = [xc, r_gate, i_gate, a_dec, a_mult, q, k, vT]

        gelu_in = [i_gate, a_dec, i_gate, a_dec]
        y_buffer = [yv2, yv2, yv, yv2]
        y_nth = [HEADS - 1, HEADS + 1, HEADS + 2, HEADS + 3]
        y_buffer_reads = [0, HEADS, HEADS + 1, HEADS + 2]

        banks = [ctx.enter_context(nc.psum_tensor(f"out{b}", [P, T], F32)) for b in range(RING)]
        ps_a = ctx.enter_context(nc.psum_tensor("ps_a", [P, T], F32))
        ps_b = ctx.enter_context(nc.psum_tensor("ps_b", [P, T], F32))
        ps_ret = ctx.enter_context(nc.psum_tensor("ps_ret", [P, T], F32))
        ps_sum = ctx.enter_context(nc.psum_tensor("ps_sum", [P, T], F32))
        ps_pair = [ps_a, ps_b]
        scores_in = [(0, ps_a[:, 0:T]), (2, ps_ret[:, 0:2 * P]),
                     (1, ps_b[:, 0:3 * P]), (3, ps_b[:, 3 * P:T])]
        SCORES_BEFORE = {0: 1, 2: 2, 1: 4, 3: 4}

        x_loaded = [sem(f"x_loaded{m}") for m in range(KC)]
        par_loaded = sem("par_loaded")
        pos_loaded = sem("pos_loaded")
        eye_loaded = sem("eye_loaded")
        mix_loaded = sem("mix_loaded")
        w_loaded = [sem(f"w_loaded{s}") for s in range(RING)]
        out_stored = sem("out_stored")
        w_hi_done = sem("w_hi_done")
        w_split = sem("w_split")
        piece_used = sem("piece_used")
        out_read = sem("out_read")
        consts = sem("consts")
        soft_step = sem("soft_step")
        soft_exp = sem("soft_exp")
        angle_step = sem("angle_step")
        trig_step = sem("trig_step")
        trig_done = sem("trig_done")
        xg_hi_done = sem("xg_hi_done")
        xg_ready = sem("xg_ready")
        sq_done = sem("sq_done")
        sumsq_step = sem("sumsq_step")
        sum_done = sem("sum_done")
        root_done = sem("root_done")
        rms_done = sem("rms_done")
        silu_done = sem("silu_done")
        h_done = sem("h_done")
        h_hi_done = sem("h_hi_done")
        h_ready = sem("h_ready")
        tables_scaled = sem("tables_scaled")
        pad_done = sem("pad_done")
        gate_w_ready = sem("gate_w_ready")
        conv0_done = sem("conv0_done")
        conv_step = sem("conv_step")
        gates_done = sem("gates_done")
        sigmoid_done = sem("sigmoid_done")
        decay_step = sem("decay_step")
        ix_done = sem("ix_done")
        mult_sq_done = sem("mult_sq_done")
        mult_done = sem("mult_done")
        u_done = sem("u_done")
        scan_done = sem("scan_done")
        rot_step = sem("rot_step")
        qk_ready = sem("qk_ready")
        scores_done = sem("scores_done")
        probs_ready = sem("probs_ready")
        turned_done = sem("turned_done")
        v_tok_ready = sem("v_tok_ready")
        ret_done = sem("ret_done")
        ret_sq_done = sem("ret_sq_done")
        head_sum_done = sem("head_sum_done")
        head_root_done = sem("head_root_done")
        head_rms_done = sem("head_rms_done")
        ret_read = sem("ret_read")
        y_done = sem("y_done")
        y_hi_done = sem("y_hi_done")
        y_ready = sem("y_ready")
        g_silu_done = sem("g_silu_done")
        gelu_done = sem("gelu_done")
        final_done = sem("final_done")

        def piece(l, quad, s):
            return l * (LAYER_Q * RING) + quad * RING + s

        def used(n):
            return n + 1 + RING

        def read(o):
            return o + 1 + RING

        def after(count):
            return count + 1

        def norm_index(l, which):
            return l * 3 + which

        def g_col(j, m):
            return par[:, bass.ds(G_AT + j * KC + m, 1)]

        def chan(at, l, c):
            return par[:, bass.ds(at + l * RC + c, 1)]

        def f32(ap):
            return ap.bitcast(F32)

        block = ctx.enter_context(nc.Block())

        X_BY_SP, X_BY_ACT, X_BY_POOL = (1,), (0, 2, 3), (4, 5, 6, 7)

        def load_x(eng, m):
            eng.dma_start(x[:, m, :], xT[m]).then_inc(x_loaded[m], 16)

        @block.sync
        def _(sp):
            def load(l, quad, s, blocks, src):
                sp.wait_ge(w_split, piece(l, quad, s) + 1)
                sp.dma_start(raw[:, s, 0:blocks, :].rearrange("p j n -> p (j n)"), src)\
                  .then_inc(w_loaded[s], 16)

            def ffn(l, a):
                with sp.Fori(0, UP_Q) as i:
                    for s in range(RING):
                        load(l, FFN_AT[a] + i, s, PIECE, w_up[a][l, i, s])
                with sp.Fori(0, DOWN_Q) as m:
                    at = 0
                    for s in range(RING):
                        load(l, FFN_AT[a] + UP_Q + m, s, DOWN[s],
                             w_down[a][l, m, :, at * P:(at + DOWN[s]) * P])
                        at += DOWN[s]

            for m in X_BY_SP:
                load_x(sp, m)
            with sp.Fori(0, DEPTH) as l:
                ffn(l, 0)
                with sp.Fori(0, PROJ_Q) as i:
                    for s in range(RING):
                        load(l, MIX_AT + i, s, PIECE, w_proj[l, i, s])
                with sp.Fori(0, MERGE_Q) as i:
                    for s in range(RING):
                        load(l, MIX_AT + PROJ_Q + i, s, PIECE, w_merge[l, i, s])
                ffn(l, 1)
            for m in range(KC):
                sp.wait_ge(final_done, m + 1)
                sp.dma_start(out[m], x[:, m, :]).then_inc(out_stored, 16)
            sp.wait_ge(out_stored, 16 * KC)

        @block.gpsimd
        def _(pool):
            pool.memset(one[:], 1.0).then_inc(w_hi_done, 1)
            pool.memset(eps[:], EPS).then_inc(w_split, RING)

            for m in X_BY_POOL:
                load_x(pool, m)
            pool.dma_start(angle[:].bitcast(I32), positions).then_inc(pos_loaded, 16)
            pool.dma_start(ident[:], eye).then_inc(eye_loaded, 16)

            hi_value = pool.alloc_register("hi_value")

            def split(l, quad, s, blocks):
                n = piece(l, quad, s)
                src = raw[:, s, 0:blocks, :].rearrange("p j n -> p (j n)")
                hi = w_hi[:, s, 0:blocks, :].rearrange("p j n -> p (j n)")
                lo = w_lo[:, s, 0:blocks, :].rearrange("p j n -> p (j n)")
                pool.wait_ge(w_loaded[s], (l * LAYER_Q + quad + 1) * 16)
                pool.wait_ge(piece_used, n + 1)
                pool.reg_add(hi_value, pool.snap(n + 1), 1)
                pool.tensor_scalar(hi, src, 1.0, 0.0, ALU.mult, ALU.add).then_inc(w_hi_done, 1)
                pool.wait_ge(w_hi_done, hi_value)
                pool.tensor_tensor(lo, src, f32(hi), ALU.subtract).then_inc(w_split, 1)

            def phase(l, first_quad, quads, blocks):
                with pool.Fori(0, quads) as i:
                    for s in range(RING):
                        split(l, first_quad + i, s, blocks[s])

            with pool.Fori(0, DEPTH) as l:
                phase(l, FFN_AT[0], UP_Q, [PIECE] * RING)
                phase(l, FFN_AT[0] + UP_Q, DOWN_Q, DOWN)
                phase(l, MIX_AT, MIX_Q, [PIECE] * RING)
                phase(l, FFN_AT[1], UP_Q, [PIECE] * RING)
                phase(l, FFN_AT[1] + UP_Q, DOWN_Q, DOWN)

        @block.tensor
        def _(pe):
            pe.sem_inc(piece_used, RING)

            def product(l, quad, s, blocks, rhs_hi, rhs_lo, bank, start, stop, ready=None):
                n = piece(l, quad, s)
                pe.wait_ge(w_split, n + 1 + RING)
                for j, (slot_block, chunk) in enumerate(blocks):
                    if ready:
                        ready(j)
                    hi, lo = w_hi[:, s, slot_block, :], w_lo[:, s, slot_block, :]
                    first, last = start and j == 0, stop and j == len(blocks) - 1
                    pe.matmul(bank[:], hi, rhs_hi[:, chunk, :], start=first, stop=False)
                    pe.matmul(bank[:], hi, rhs_lo[:, chunk, :], start=False, stop=False)
                    mm = pe.matmul(bank[:], lo, rhs_hi[:, chunk, :], start=False, stop=last)
                mm.then_inc(piece_used, 1)

            all_chunks = [(j, j) for j in range(KC)]

            def x_product(l, quad, s, o, ready=None):
                pe.wait_ge(out_read, o + 1)
                product(l, quad, s, all_chunks, xg_hi, xg_lo, banks[s], True, True, ready)

            def sum_squares(j):
                pe.wait_ge(sumsq_step, (KC + 1) * (j + 1))
                pe.matmul(ps_sum[:], ones[:], sumsq[:], start=True, stop=True).then_inc(sum_done, 1)

            def first_quad(l, quad, o, j):
                def chunk_ready(kc):
                    pe.wait_ge(xg_ready, KC * j + kc + 1)
                x_product(l, quad, 0, o, chunk_ready)
                sum_squares(j)
                for s in range(1, RING):
                    x_product(l, quad, s, o + s)

            def ffn(l, a):
                quad, o, j = FFN_AT[a], l * LAYER_O + FFN_O_AT[a], norm_index(l, NORM_OF_FFN[a])
                first_quad(l, quad, o, j)
                with pe.Fori(1, UP_Q) as i:
                    for s in range(RING):
                        x_product(l, quad + i, s, o + i * RING + s)
                h_base = l * (2 * FC) + a * FC
                with pe.Fori(0, DOWN_Q // RING) as i:
                    for b in range(RING):
                        pe.wait_ge(out_read, o + RING * UP_Q + i * RING + b + 1)
                        at = 0
                        for s in range(RING):
                            def hidden_ready(j, at=at):
                                if at + j == 0:
                                    pe.wait_ge(h_ready, after(h_base + FC - 2))
                                elif at + j >= FC - 2:
                                    pe.wait_ge(h_ready, after(h_base + at + j + 1))
                            product(l, quad + UP_Q + i * RING + b, s,
                                    [(jj, at + jj) for jj in range(DOWN[s])], h_hi, h_lo,
                                    banks[b], s == 0, s == RING - 1, hidden_ready)
                            at += DOWN[s]

            def head_sum(l, h):
                pe.wait_ge(ret_sq_done, l * HEADS + h + 1)
                pe.matmul(ps_sum[:], ones[:], square[:], start=True, stop=True)\
                  .then_inc(head_sum_done, 1)

            def head_step(l, h, tail):
                quad, o = MIX_AT + 1 + h, l * LAYER_O + MIX_O_AT + (1 + h) * RING
                x_product(l, quad, 0, o)
                if tail:
                    head_sum(l, h - 1)
                x_product(l, quad, 1, o + 1)
                pe.wait_ge(gate_w_ready, l * RC + h + 1)
                pe.wait_ge(conv_step, l * (3 * RC) + h * 3 + 3)
                for n in range(2):
                    pe.matmul(ps_pair[n][:], gate_now[:, n, :], xc[:], start=True, stop=True)\
                      .then_inc(gates_done, 1)
                x_product(l, quad, 2, o + 2)
                pe.wait_ge(qk_ready, after((l * HEADS + h) * 2 + 2))
                pe.wait_ge(sigmoid_done, (l * RC + h) * 2 + 2)
                pe.wait_ge(ret_read, after(l * HEADS + h))
                for j, place in scores_in:
                    pe.matmul(place, k[:, j * P:(j + 1) * P],
                              q[:, j * P:T], start=True, stop=True).then_inc(scores_done, 1)
                pe.wait_ge(out_read, read(o + 2))
                pe.wait_ge(eye_loaded, 16)
                if tail:
                    pe.wait_ge(head_root_done, l * HEADS + h)
                for j in range(TC):
                    tr = pe.transpose(ps_sum[:, j * P:(j + 1) * P], vT[:, j * P:(j + 1) * P], ident[:])
                tr.then_inc(turned_done, 1)
                x_product(l, quad, 3, o + 3)
                pe.wait_ge(v_tok_ready, l * HEADS + h + 1)
                pe.wait_ge(probs_ready, (l * HEADS + h) * TC + TC)
                at = 0
                for j in range(TC):
                    mm = pe.matmul(ps_ret[:, j * P:T], v_tok[:, j, :], probs[:, at:at + T - j * P],
                                   start=j == 0, stop=j == TC - 1)
                    at += T - j * P
                mm.then_inc(ret_done, 1)

            def mix(l):
                quad, o = MIX_AT, l * LAYER_O + MIX_O_AT
                first_quad(l, quad, o, norm_index(l, NORM_OF_MIX))
                head_step(l, 0, False)
                with pe.Fori(1, HEADS) as h:
                    head_step(l, h, True)
                x_product(l, quad + PROJ_Q - 1, 0, o + RING * (PROJ_Q - 1))
                head_sum(l, HEADS - 1)
                for s in range(1, RING):
                    x_product(l, quad + PROJ_Q - 1, s, o + RING * (PROJ_Q - 1) + s)
                order = [RC, RC + 1, RC + 2, 0, RC + 3, 1, 2, 3]
                with pe.Fori(0, MERGE_Q) as i:
                    for s in range(RING):
                        pe.wait_ge(out_read, o + RING * (PROJ_Q + i) + s + 1)
                        def y_chunk_ready(j):
                            if j == 0 or j >= 3:
                                pe.wait_ge(y_ready, after(l * YS + max(j + 1, 3)))
                        product(l, quad + PROJ_Q + i, s, [(c, c) for c in order], y_hi, y_lo,
                                banks[s], True, True, y_chunk_ready)

            pe.wait_ge(consts, 2)
            with pe.Fori(0, DEPTH) as l:
                ffn(l, 0)
                mix(l)
                ffn(l, 1)
            sum_squares(NORMS - 1)

        @block.scalar
        def _(act):
            act.dma_start(par[:], params).then_inc(par_loaded, 16)
            for m in X_BY_ACT:
                load_x(act, m)

            def xg_high(j, m):
                act.activation(xg_hi[:, m, :], x[:, m, :], ACT.Identity, scale=g_col(j, m))\
                   .then_inc(xg_hi_done, 1)

            def x_updates(j, o):
                with act.Fori(0, KC) as m:
                    act.wait_ge(out_read, read(o + m))
                    act.wait_ge(sumsq_step, (KC + 1) * j + m + 1)
                    act.activation(square[:], x[:, m, :], ACT.Square).then_inc(sq_done, 1)
                    xg_high(j, m)

            def root(j):
                act.wait_ge(sum_done, j + 1)
                act.activation(square[:], ps_sum[:], ACT.Sqrt, scale=1.0 / D, bias=eps[:])\
                   .then_inc(root_done, 1)

            def up(l, a):
                root(norm_index(l, NORM_OF_FFN[a]))
                base = l * (2 * FC) + a * FC
                o = l * LAYER_O + FFN_O_AT[a]
                with act.Fori(0, FC) as f:
                    act.wait_ge(out_read, read(o + 2 * f))
                    act.activation(tmp0[:], tmp0[:], ACT.Silu).then_inc(silu_done, 1)
                    act.wait_ge(h_done, base + f + 1)
                    act.activation(h_hi[:, f, :], tmp1[:], ACT.Copy).then_inc(h_hi_done, 1)

            def trig(l):
                act.wait_ge(trig_step, l * TRIG_STEPS + TRIG_STEPS)
                act.activation(sin[0:64, :], cos[0:64, :], ACT.Sin).then_inc(trig_done, 1)
                act.activation(sin[64:P, :], cos[64:P, :], ACT.Sin, scale=-1.0).then_inc(trig_done, 1)
                act.wait_ge(trig_done, 3 * l + 2)
                act.activation(cos[:], tmp1[:], ACT.Sin, scale=-1.0, bias=half_pi[:])\
                   .then_inc(trig_done, 1)

            def head_square(l, h):
                act.wait_ge(ret_done, l * HEADS + h + 1)
                act.activation(square[:], ps_ret[:], ACT.Square).then_inc(ret_sq_done, 1)

            def head_root(l, h):
                act.wait_ge(head_sum_done, l * HEADS + h + 1)
                act.activation(head_rms[:], ps_sum[:], ACT.Sqrt, scale=1.0 / DH, bias=eps[:])\
                   .then_inc(head_root_done, 1)

            def y_high(l, nth, chunk, y=yv):
                act.wait_ge(y_done, l * YS + nth + 1)
                act.activation(y_hi[:, chunk, :], y[:], ACT.Copy).then_inc(y_hi_done, 1)

            def head_step(l, h, tail):
                if tail:
                    head_square(l, h - 1)
                act.wait_ge(out_read, read(l * LAYER_O + MIX_O_AT + h))
                act.activation(xc[:], xr[:, h, TAPS - 1:], ACT.Identity,
                               scale=par[:, bass.ds(CONV_W_AT + (l * TAPS + TAPS - 1) * RC + h, 1)],
                               bias=chan(CONV_B_AT, l, h)).then_inc(conv0_done, 1)
                if tail:
                    head_root(l, h - 1)
                    y_high(l, h - 1, RC + h - 1)
                act.wait_ge(scan_done, after(l * RC + h))
                act.wait_ge(gates_done, (l * RC + h) * 2 + 1)
                act.activation(r_gate[:], ps_a[:], ACT.Sigmoid, bias=chan(GATE_A_B_AT, l, h))\
                   .then_inc(sigmoid_done, 1)
                act.wait_ge(gates_done, (l * RC + h) * 2 + 2)
                act.activation(i_gate[:], ps_b[:], ACT.Sigmoid, bias=chan(GATE_X_B_AT, l, h))\
                   .then_inc(sigmoid_done, 1)
                act.wait_ge(sigmoid_done, (l * RC + h) * 2 + 1)
                act.activation(a_dec[:], r_gate[:], ACT.Exp, scale=lru_neg[:, bass.ds(l * RC + h, 1)])\
                   .then_inc(decay_step, 1)
                act.activation(a_mult[:], r_gate[:], ACT.Tanh, scale=lru_pos[:, bass.ds(l * RC + h, 1)])\
                   .then_inc(decay_step, 1)
                act.wait_ge(decay_step, (l * RC + h) * 3 + 2)
                act.activation(r_gate[:], a_dec[:], ACT.Square).then_inc(decay_step, 1)
                act.wait_ge(turned_done, l * HEADS + h + 1)
                act.activation(v_tok[:].rearrange("p j n -> p (j n)"), ps_sum[:], ACT.Copy)\
                   .then_inc(v_tok_ready, 1)
                act.wait_ge(mult_sq_done, l * RC + h + 1)
                act.activation(a_mult[:], a_mult[:], ACT.Sqrt).then_inc(mult_done, 1)
                act.wait_ge(out_read, read(l * LAYER_O + MIX_O_AT + (1 + h) * RING + 3))
                act.activation(g_silu[:], g_silu[:], ACT.Silu).then_inc(g_silu_done, 1)

            def gelu(l, c):
                act.wait_ge(out_read, read(l * LAYER_O + MIX_O_AT + RING * (PROJ_Q - 1) + c))
                act.activation(gelu_in[c][:], gelu_in[c][:], ACT.Gelu_apprx_tanh)\
                   .then_inc(gelu_done, 1)

            def mix(l):
                act.wait_ge(piece_used, used(piece(l, MIX_AT - 1, RING - 1)))
                act.dma_start(dec[:], decay).then_inc(mix_loaded, 16)
                act.dma_start(gate_w[:], gates[l]).then_inc(mix_loaded, 16)
                root(norm_index(l, NORM_OF_MIX))
                head_step(l, 0, False)
                with act.Fori(1, HEADS) as h:
                    head_step(l, h, True)
                head_square(l, HEADS - 1)
                gelu(l, 0)
                y_high(l, HEADS - 1, 0, y_buffer[0])
                head_root(l, HEADS - 1)
                gelu(l, 1)
                y_high(l, HEADS, RC + HEADS - 1)
                y_high(l, HEADS + 1, 1, y_buffer[1])
                for c in range(2, RC):
                    gelu(l, c)
                    y_high(l, HEADS + c, c, y_buffer[c])
                x_updates(norm_index(l, NORM_OF_MIX) + 1, l * LAYER_O + MIX_O_AT + RING * PROJ_Q)

            act.wait_ge(par_loaded, 16)
            for m in range(KC):
                act.wait_ge(x_loaded[m], 16)
                xg_high(0, m)
            for m in range(KC):
                act.activation(first_square[m][:], x[:, m, :], ACT.Square).then_inc(sq_done, 1)
            act.wait_ge(soft_step, 1)
            act.activation(soft[:, 1, :], soft[:, 0, :], ACT.Exp, scale=-1.0).then_inc(soft_exp, 1)
            act.wait_ge(consts, 2)
            with act.Fori(0, DEPTH) as l:
                up(l, 0)
                trig(l)
                x_updates(norm_index(l, NORM_OF_FFN[0]) + 1, l * LAYER_O + FFN_O_AT[0] + RING * UP_Q)
                mix(l)
                up(l, 1)
                x_updates(norm_index(l, NORM_OF_FFN[1]) + 1, l * LAYER_O + FFN_O_AT[1] + RING * UP_Q)
            root(NORMS - 1)

        @block.vector
        def _(dve):
            for credit in (h_ready, qk_ready, scan_done, ret_read, y_ready):
                dve.sem_inc(credit, 1)
            dve.memset(ones[:], 1.0).then_inc(consts, 1)
            dve.memset(half_pi[:], TWO_PI / 4).then_inc(consts, 1)
            dve.memset(sumsq[:], 0.0).then_inc(sumsq_step, 1)
            dve.memset(tmp1[:], 0.0).then_inc(out_read, RING)

            def clear_sum():
                dve.memset(sumsq[:], 0.0).then_inc(sumsq_step, 1)

            def norm_prep(j, m):
                add_square(j, m, square)
                xg_low(j, m)

            def add_square(j, m, x_squared):
                dve.wait_ge(sq_done, KC * j + m + 1)
                dve.wait_ge(sumsq_step, (KC + 1) * j + m + 1)
                dve.tensor_tensor(sumsq[:], sumsq[:], x_squared[:], ALU.add).then_inc(sumsq_step, 1)

            def xg_low(j, m):
                dve.wait_ge(xg_hi_done, KC * j + m + 1)
                dve.scalar_tensor_tensor(xg_lo[:, m, :], x[:, m, :], g_col(j, m), f32(xg_hi[:, m, :]),
                                         ALU.mult, ALU.subtract).then_inc(xg_ready, 1)

            def factor(j):
                dve.wait_ge(root_done, j + 1)
                dve.reciprocal(rms[:], square[:]).then_inc(rms_done, 1)

            def residual(l, quad, last_slot, o, j, m, bank, scale):
                dve.wait_ge(piece_used, used(piece(l, quad, last_slot)))
                dve.scalar_tensor_tensor(x[:, m, :], bank[:], scale, x[:, m, :], ALU.mult, ALU.add)\
                   .then_inc(out_read, 1)
                norm_prep(j, m)

            def ffn(l, a):
                quad, o, j = FFN_AT[a], l * LAYER_O + FFN_O_AT[a], norm_index(l, NORM_OF_FFN[a])
                base = l * (2 * FC) + a * FC
                factor(j)
                with dve.Fori(0, UP_Q) as i:
                    for b in range(2):
                        f = i * 2 + b
                        dve.wait_ge(rms_done, j + 1)
                        dve.wait_ge(piece_used, used(piece(l, quad + i, 2 * b)))
                        dve.tensor_tensor(tmp0[:], banks[2 * b][:], rms[:], ALU.mult)\
                           .then_inc(out_read, 1)
                        dve.wait_ge(h_ready, after(base + f))
                        dve.wait_ge(piece_used, used(piece(l, quad + i, 2 * b + 1)))
                        dve.tensor_tensor(tmp1[:], banks[2 * b + 1][:], rms[:], ALU.mult)\
                           .then_inc(out_read, 1)
                        dve.wait_ge(silu_done, base + f + 1)
                        dve.wait_ge(out_read, read(o + i * RING + 2 * b + 1))
                        dve.tensor_tensor(tmp1[:], tmp0[:], tmp1[:], ALU.mult).then_inc(h_done, 1)
                        dve.wait_ge(h_hi_done, base + f + 1)
                        dve.wait_ge(h_done, base + f + 1)
                        dve.tensor_tensor(h_lo[:, f, :], tmp1[:], f32(h_hi[:, f, :]), ALU.subtract)\
                           .then_inc(h_ready, 1)
                clear_sum()
                if a == 0:
                    trig(l)
                with dve.Fori(0, DOWN_Q // RING) as i:
                    for b in range(RING):
                        residual(l, quad + UP_Q + i * RING + b, RING - 1,
                                 o + RING * UP_Q + i * RING + b, j + 1, i * RING + b, banks[b], 0.5)

            def trig(l):
                n, n_hi, y = tmp0, tmp1, cos
                step = [0]

                def did(ins):
                    ins.then_inc(trig_step, 1)
                    step[0] += 1
                    if step[0] < TRIG_STEPS:
                        dve.wait_ge(trig_step, l * TRIG_STEPS + step[0])

                dve.wait_ge(h_ready, after(l * (2 * FC) + FC))
                did(dve.tensor_scalar(n[:], angle[:], 1 / TWO_PI, ROUND, ALU.mult, ALU.add))
                did(dve.tensor_scalar(n[:], n[:], -ROUND, None, ALU.add))
                did(dve.tensor_scalar(n_hi[:], n[:], 1 / TURN, ROUND, ALU.mult, ALU.add))
                did(dve.tensor_scalar(n_hi[:], n_hi[:], -ROUND, None, ALU.add))
                did(dve.scalar_tensor_tensor(n[:], n_hi[:], -TURN, n[:], ALU.mult, ALU.add))
                src = angle
                for part in TURN_PARTS:
                    for count, size in ((n_hi, TURN), (n, 1.0)):
                        did(dve.scalar_tensor_tensor(y[:], count[:], -part * size, src[:],
                                                     ALU.mult, ALU.add))
                        src = y
                did(dve.tensor_scalar(n[:], y[:], 1 / TWO_PI, ROUND, ALU.mult, ALU.add))
                did(dve.tensor_scalar(n[:], n[:], -ROUND, None, ALU.add))
                did(dve.scalar_tensor_tensor(y[:], n[:], -TWO_PI, y[:], ALU.mult, ALU.add))
                did(dve.tensor_scalar(y[:], y[:], PI_BELOW, -PI_BELOW, ALU.min, ALU.max))
                did(dve.scalar_tensor_tensor(n_hi[:], y[:], -1.0, y[:], ALU.mult, ALU.max))
                assert step[0] == TRIG_STEPS

            def rotary(l, h, which, quad, o, dst):
                bank = banks[which]
                nth = (l * HEADS + h) * 2 + which
                dve.wait_ge(qk_ready, after(nth))
                dve.wait_ge(piece_used, used(piece(l, quad, which)))
                dve.tensor_tensor(tmp0[:], bank[:], cos_r[:], ALU.mult).then_inc(rot_step, 1)
                dve.tensor_tensor(tmp1[0:64, :], bank[64:P, :], sin_r[64:P, :], ALU.mult)\
                   .then_inc(rot_step, 1)
                dve.tensor_tensor(tmp1[64:P, :], bank[0:64, :], sin_r[0:64, :], ALU.mult)\
                   .then_inc(out_read, 1)
                dve.wait_ge(rot_step, nth * 2 + 2)
                dve.wait_ge(out_read, read(o + which))
                dve.tensor_tensor(dst[:], tmp0[:], tmp1[:], ALU.add).then_inc(qk_ready, 1)

            def y_low(l, nth, chunk, y=yv):
                dve.wait_ge(y_hi_done, l * YS + nth + 1)
                dve.tensor_tensor(y_lo[:, chunk, :], y[:], f32(y_hi[:, chunk, :]), ALU.subtract)\
                   .then_inc(y_ready, 1)

            def head_factor(l, h):
                dve.wait_ge(head_root_done, l * HEADS + h + 1)
                dve.reciprocal(head_rms[:], head_rms[:]).then_inc(head_rms_done, 1)

            def head_out(l, h, yv_reads):
                dve.wait_ge(head_rms_done, l * HEADS + h + 1)
                dve.wait_ge(y_ready, after(yv_reads))
                dve.tensor_tensor(yv[:], ps_ret[:], head_rms[:], ALU.mult).then_inc(ret_read, 1)
                dve.wait_ge(ret_read, after(l * HEADS + h + 1))
                dve.wait_ge(g_silu_done, l * HEADS + h + 1)
                dve.tensor_tensor(yv[:], yv[:], g_silu[:], ALU.mult).then_inc(y_done, 1)

            def head_step(l, h, tail):
                quad, o = MIX_AT + 1 + h, l * LAYER_O + MIX_O_AT + (1 + h) * RING
                dve.tensor_copy(gate_now[:], gate_w[:, :, h, :]).then_inc(gate_w_ready, 1)
                dve.wait_ge(conv0_done, l * RC + h + 1)
                for t in range(TAPS - 1):
                    if t:
                        dve.wait_ge(conv_step, (l * RC + h) * 3 + t)
                    dve.scalar_tensor_tensor(
                        xc[:], xr[:, h, t:t + T],
                        par[:, bass.ds(CONV_W_AT + (l * TAPS + t) * RC + h, 1)], xc[:],
                        ALU.mult, ALU.add).then_inc(conv_step, 1)
                rotary(l, h, 0, quad, o, q)
                if tail:
                    head_factor(l, h - 1)
                    head_out(l, h - 1, l * YS + (h - 1))
                    y_low(l, h - 1, RC + h - 1)
                rotary(l, h, 1, quad, o, k)
                dve.wait_ge(piece_used, used(piece(l, quad, 2)))
                dve.tensor_tensor(vT[:], banks[2][:], rms[:], ALU.mult).then_inc(out_read, 1)
                for j, place in scores_in:
                    at = sum(T - i * P for i in range(j))
                    dve.wait_ge(scores_done, (l * HEADS + h) * TC + SCORES_BEFORE[j])
                    dve.tensor_tensor(probs[:, at:at + T - j * P], place,
                                      dec[:, h, 0:T - j * P], ALU.mult).then_inc(probs_ready, 1)
                dve.wait_ge(sigmoid_done, (l * RC + h) * 2 + 2)
                dve.tensor_tensor(i_gate[:], i_gate[:], xc[:], ALU.mult).then_inc(ix_done, 1)
                dve.wait_ge(decay_step, (l * RC + h) * 3 + 3)
                dve.scalar_tensor_tensor(a_mult[:], r_gate[:], 1.0, a_mult[:], ALU.add, ALU.mult)\
                   .then_inc(mult_sq_done, 1)
                dve.wait_ge(mult_done, l * RC + h + 1)
                dve.wait_ge(ix_done, l * RC + h + 1)
                dve.tensor_tensor(i_gate[:], i_gate[:], a_mult[:], ALU.mult).then_inc(u_done, 1)
                dve.wait_ge(u_done, l * RC + h + 1)
                dve.tensor_tensor_scan(xr[:, h, 0:T], a_dec[:], i_gate[:], 0.0, ALU.mult, ALU.add)\
                   .then_inc(scan_done, 1)
                dve.wait_ge(piece_used, used(piece(l, quad, 3)))
                dve.tensor_tensor(g_silu[:], banks[3][:], rms[:], ALU.mult).then_inc(out_read, 1)

            def gate_out(l, c):
                dve.wait_ge(piece_used, used(piece(l, MIX_AT + PROJ_Q - 1, c)))
                dve.wait_ge(scan_done, after(l * RC + RC))
                if c >= 2:
                    dve.wait_ge(y_done, l * YS + y_nth[c - 2] + 1)
                dve.tensor_tensor(gelu_in[c][:], banks[c][:], rms[:], ALU.mult).then_inc(out_read, 1)

            def rnn_out(l, c):
                dve.wait_ge(gelu_done, l * RC + c + 1)
                dve.wait_ge(y_ready, after(l * YS + y_buffer_reads[c]))
                dve.tensor_tensor(y_buffer[c][:], gelu_in[c][:], xr[:, c, 0:T], ALU.mult)\
                   .then_inc(y_done, 1)

            def rnn_low(l, c):
                dve.wait_ge(y_done, l * YS + y_nth[c] + 1)
                y_low(l, y_nth[c], c, y_buffer[c])

            def mix(l):
                quad, o, j = MIX_AT, l * LAYER_O + MIX_O_AT, norm_index(l, NORM_OF_MIX)
                factor(j)
                dve.wait_ge(rms_done, j + 1)
                dve.wait_ge(trig_done, 3 * (l + 1))
                dve.tensor_tensor(cos_r[:], cos[:], rms[:], ALU.mult).then_inc(tables_scaled, 1)
                dve.tensor_tensor(sin_r[:], sin[:], rms[:], ALU.mult).then_inc(tables_scaled, 1)
                dve.memset(xr[:, :, 0:TAPS - 1], 0.0).then_inc(pad_done, 1)
                for c in range(RC):
                    dve.wait_ge(piece_used, used(piece(l, quad, c)))
                    dve.tensor_tensor(xr[:, c, TAPS - 1:], banks[c][:], rms[:], ALU.mult)\
                       .then_inc(out_read, 1)
                dve.wait_ge(pad_done, l + 1)
                dve.wait_ge(tables_scaled, 2 * (l + 1))
                dve.wait_ge(mix_loaded, 32 * (l + 1))
                head_step(l, 0, False)
                with dve.Fori(1, HEADS) as h:
                    head_step(l, h, True)
                gate_out(l, 0)
                rnn_out(l, 0)
                rnn_low(l, 0)
                head_factor(l, HEADS - 1)
                gate_out(l, 1)
                head_out(l, HEADS - 1, l * YS + HEADS)
                rnn_out(l, 1)
                y_low(l, HEADS, RC + HEADS - 1)
                rnn_low(l, 1)
                for c in range(2, RC):
                    gate_out(l, c)
                    rnn_out(l, c)
                    rnn_low(l, c)
                clear_sum()
                with dve.Fori(0, MERGE_Q) as i:
                    for b in range(RING):
                        residual(l, quad + PROJ_Q + i, b, o + RING * (PROJ_Q + i) + b,
                                 j + 1, i * RING + b, banks[b], 1.0)

            lam = par[:, LAM_AT:LAM_AT + DEPTH * RC]
            magnitude, expo, series, s2 = (soft[:, i, :] for i in range(4))
            step = [0]

            def did(ins):
                ins.then_inc(soft_step, 1)
                step[0] += 1
                dve.wait_ge(soft_step, step[0])

            dve.wait_ge(par_loaded, 16)
            did(dve.scalar_tensor_tensor(magnitude, lam, -1.0, lam, ALU.mult, ALU.max))
            for m in range(KC):
                xg_low(0, m)
            for m in range(KC):
                add_square(0, m, first_square[m])
            dve.wait_ge(soft_exp, 1)
            did(dve.tensor_scalar(magnitude, expo, 2.0, None, ALU.add))
            did(dve.reciprocal(magnitude, magnitude))
            did(dve.tensor_tensor(expo, expo, magnitude, ALU.mult))
            did(dve.tensor_tensor(s2, expo, expo, ALU.mult))
            did(dve.tensor_scalar(series, s2, 1.0 / 17, None, ALU.mult))
            for odd in (15, 13, 11, 9, 7, 5, 3):
                did(dve.scalar_tensor_tensor(series, series, 1.0 / odd, s2, ALU.add, ALU.mult))
            did(dve.scalar_tensor_tensor(series, series, 1.0, expo, ALU.add, ALU.mult))
            did(dve.tensor_scalar(magnitude, lam, -1.0, 0.0, ALU.mult, ALU.max))
            did(dve.scalar_tensor_tensor(series, series, 2.0, magnitude, ALU.mult, ALU.add))
            did(dve.tensor_scalar(lru_pos[:], series, LRU_C, None, ALU.mult))
            did(dve.tensor_scalar(lru_neg[:], series, -LRU_C, None, ALU.mult))
            dve.wait_ge(pos_loaded, 16)
            dve.tensor_copy(tmp0[:], angle[:].bitcast(I32)).then_inc(angle_step, 1)
            dve.wait_ge(angle_step, 1)
            dve.tensor_scalar(angle[:], tmp0[:], par[:, FREQ_AT:FREQ_AT + 1], None, ALU.mult)\
               .then_inc(angle_step, 1)
            dve.wait_ge(angle_step, 2)

            with dve.Fori(0, DEPTH) as l:
                ffn(l, 0)
                mix(l)
                ffn(l, 1)
            factor(NORMS - 1)
            dve.wait_ge(rms_done, NORMS)
            for m in range(KC):
                dve.scalar_tensor_tensor(x[:, m, :], x[:, m, :], g_col(NORMS - 1, m), rms[:],
                                         ALU.mult, ALU.mult).then_inc(final_done, 1)


def kernel(**inputs):
    import numpy as _np
    import concourse.bacc as _bacc
    from concourse import mybir as _mybir
    from concourse.bass_utils import run_bass_kernel_spmd as _run

    a = {name: _np.asarray(value) for name, value in inputs.items()}

    def chunks(v):
        return _np.moveaxis(v.reshape(-1, P), -1, 0)

    def up_pieces(w):
        w = w.reshape(DEPTH, KC, P, 2, FC, P)
        return w.transpose(0, 4, 3, 2, 1, 5).reshape(DEPTH, UP_Q, RING, P, KC * P)

    def down_pieces(w):
        return w.reshape(DEPTH, FC, P, KC, P).transpose(0, 3, 2, 1, 4).reshape(DEPTH, KC, P, FF)

    def proj_pieces(w):
        w = w.reshape(DEPTH, KC, P, 6, RC, P)
        by_chunk = w.transpose(0, 3, 4, 2, 1, 5)
        heads = by_chunk[:, 2:6].transpose(0, 2, 1, 3, 4, 5)
        order = _np.concatenate([by_chunk[:, 0:1], heads, by_chunk[:, 1:2]], axis=1)
        return order.reshape(DEPTH, PROJ_Q, RING, P, KC * P)

    def merge_pieces(w):
        return w.reshape(DEPTH, KC, P, KC, P).transpose(0, 3, 2, 1, 4)\
                .reshape(DEPTH, MERGE_Q, RING, P, KC * P)

    norms = _np.concatenate([_np.stack([a["norm_ffn1"], a["norm_mix"], a["norm_ffn2"]], axis=1)
                             .reshape(-1, D), a["norm_final"].reshape(1, D)])
    freq = (10000.0 ** (-_np.arange(DH // 2) / (DH // 2))).astype(_np.float32)
    params = _np.concatenate([
        chunks(norms), chunks(a["conv_w"]), chunks(a["conv_b"]), chunks(a["gate_a_b"]),
        chunks(a["gate_x_b"]), chunks(a["lru_lambda"]), _np.concatenate([freq, freq])[:, None]],
        axis=1)
    half = P // 2
    gates = _np.zeros((DEPTH, P, 2, RC, P), a["gate_a_w"].dtype)
    for n, name in enumerate(("gate_a_w", "gate_x_w")):
        blocks = a[name].reshape(DEPTH, RC, 2, half, half)
        for b in range(2):
            gates[:, b * half:(b + 1) * half, n, :, b * half:(b + 1) * half] = \
                blocks[:, :, b].transpose(0, 2, 1, 3)
    gamma = 1.0 - 2.0 ** (-5.0 - _np.arange(HEADS))
    rel = _np.arange(T)[None, :] - _np.arange(P)[:, None]
    decay = _np.where(rel[:, None, :] >= 0,
                      gamma[None, :, None] ** _np.maximum(rel, 0)[:, None, :], 0.0) * DH ** -0.5

    arrays = {
        "in_x": a["x"].reshape(T, KC, P).transpose(1, 2, 0),
        "in_positions": _np.repeat(a["positions"].reshape(1, T), P, axis=0),
        "in_params": params,
        "in_up0": up_pieces(a["w_ffn1_in"]),
        "in_up1": up_pieces(a["w_ffn2_in"]),
        "in_down0": down_pieces(a["w_ffn1_out"]),
        "in_down1": down_pieces(a["w_ffn2_out"]),
        "in_proj": proj_pieces(a["w_in"]),
        "in_merge": merge_pieces(a["w_out"]),
        "in_gates": gates,
        "in_decay": decay.astype(_np.float32),
        "in_eye": _np.eye(P, dtype=_np.float32),
    }
    arrays = {name: _np.ascontiguousarray(v) for name, v in arrays.items()}
    nc = _bacc.Bacc("TRN2", target_bir_lowering=False, num_devices=1)
    t = {name: nc.dram_tensor(name, v.shape, _mybir.dt.from_np(v.dtype), kind="ExternalInput").ap()
         for name, v in arrays.items()}
    out = nc.dram_tensor("out_x", (KC, P, T), _mybir.dt.float32, kind="ExternalOutput").ap()
    build(nc, t["in_x"], t["in_positions"], t["in_params"], (t["in_up0"], t["in_up1"]),
          (t["in_down0"], t["in_down1"]), t["in_proj"], t["in_merge"], t["in_gates"],
          t["in_decay"], t["in_eye"], out)
    r = _run(nc, [arrays], core_ids=[0])
    got = r.results[0]["out_x"]
    return _np.ascontiguousarray(got.reshape(D, T).T).reshape(1, T, D)
```

```python
from contextlib import ExitStack

import concourse.bass as bass
from concourse import mybir

F32 = mybir.dt.float32
F32R = mybir.dt.float32r
I32 = mybir.dt.int32
ALU = mybir.AluOpType
ACT = mybir.ActivationFunctionType

P = 128
T = 512
D = 1024
DEPTH = 2
FF = 2816
HEADS = 4
DH = 128
LRU_C = 8.0
EPS = 1e-6
KC = D // P
FC = FF // P
TC = T // P
RC = 4

RING = 4
PIECE = KC
DOWN = (6, 6, 5, 5)
assert sum(DOWN) == FC

UP_Q, DOWN_Q, PROJ_Q, MERGE_Q = 2 * FC // RING, KC, 6, KC // RING
FFN_Q, MIX_Q = UP_Q + DOWN_Q, PROJ_Q + MERGE_Q
LAYER_Q = 2 * FFN_Q + MIX_Q
FFN_AT = (0, FFN_Q + MIX_Q)
MIX_AT = FFN_Q
FFN_O, MIX_O = RING * UP_Q + KC, RING * PROJ_Q + KC
LAYER_O = 2 * FFN_O + MIX_O
FFN_O_AT = (0, FFN_O + MIX_O)
MIX_O_AT = FFN_O
NORMS = 3 * DEPTH + 1
NORM_OF_FFN = (0, 2)
NORM_OF_MIX = 1
YS = HEADS + RC

G_AT = 0
CONV_W_AT = G_AT + NORMS * KC
CONV_B_AT = CONV_W_AT + DEPTH * 4 * RC
GATE_A_B_AT = CONV_B_AT + DEPTH * RC
GATE_X_B_AT = GATE_A_B_AT + DEPTH * RC
LAM_AT = GATE_X_B_AT + DEPTH * RC
FREQ_AT = LAM_AT + DEPTH * RC
NPAR = FREQ_AT + 1
TAPS = 4

TWO_PI_UNIT = 10 ** 36
TWO_PI_UNITS = 6283185307179586476925286766559005768
TWO_PI = TWO_PI_UNITS / TWO_PI_UNIT
PI_BELOW = 3.1415925
TURN = 2048.0
ROUND = 1.5 * 2.0 ** 23


def two_pi_parts():
    parts, taken, last = [], 0, 52
    for bits in (8, 19, 30, 41):
        digits = (TWO_PI_UNITS << bits) // TWO_PI_UNIT << (last - bits)
        parts.append((digits - taken) / 2.0 ** last)
        taken = digits
    return parts + [((TWO_PI_UNITS << last) // TWO_PI_UNIT - taken) / 2.0 ** last]


TURN_PARTS = two_pi_parts()
TRIG_STEPS = 20
WARM_UP, WARM_SUM, WARM_SPREAD = 4, 3, 2


def build(nc, xT, positions, params, w_up, w_down, w_proj, w_merge, gates, decay, eye, out):
    ctx = ExitStack()
    with ctx:
        def sb(name, shape, dt=F32):
            return ctx.enter_context(nc.sbuf_tensor(name, shape, dt))

        def sem(name):
            return ctx.enter_context(nc.semaphore(name))

        x = sb("x_sb", [P, KC, T])
        xg_hi = sb("xg_hi", [P, KC, T], F32R)
        xg_lo = sb("xg_lo", [P, KC, T], F32R)
        raw = sb("raw", [P, RING, PIECE, P])
        w_hi = sb("w_hi", [P, RING, PIECE, P], F32R)
        w_lo = sb("w_lo", [P, RING, PIECE, P], F32R)
        rms = sb("rms", [P, T])
        square = sb("square", [P, T])
        sumsq = sb("sumsq", [P, T])
        tmp0 = sb("tmp0", [P, T])
        tmp1 = sb("tmp1", [P, T])
        cos = sb("cos", [P, T])
        sin = sb("sin", [P, T])
        angle = sb("angle", [P, T])
        par = sb("par", [P, NPAR])
        ones = sb("ones", [P, P], F32R)
        sum_hi = sb("sum_hi", [P, T], F32R)
        sum_lo = sb("sum_lo", [P, T], F32R)
        ident = sb("ident", [P, P])
        eps = sb("eps", [P, 1])
        token_rms = sb("token_rms", [P, TC])
        one = sb("one", [P, 1])
        half_pi = sb("half_pi", [P, 1])
        lru_pos = sb("lru_pos", [P, DEPTH * RC])
        lru_neg = sb("lru_neg", [P, DEPTH * RC])
        soft = sb("soft", [P, 4, DEPTH * RC])

        hidden = ExitStack()
        h_hi = hidden.enter_context(nc.sbuf_tensor("h_hi", [P, FC, T], F32R))
        h_lo = hidden.enter_context(nc.sbuf_tensor("h_lo", [P, FC, T], F32R))
        hidden.close()
        y_hi = sb("y_hi", [P, YS, T], F32R)
        y_lo = sb("y_lo", [P, YS, T], F32R)
        dec = sb("dec", [P, HEADS, T])
        gate_w = sb("gate_w", [P, 2, RC, P])
        gate_hi = sb("gate_hi", [P, 2, P], F32R)
        gate_lo = sb("gate_lo", [P, 2, P], F32R)
        xr = sb("xr", [P, RC, TAPS - 1 + T])
        xc = sb("xc", [P, T])
        xc_hi = sb("xc_hi", [P, T], F32R)
        xc_lo = sb("xc_lo", [P, T], F32R)
        r_gate = sb("r_gate", [P, T])
        i_gate = sb("i_gate", [P, T])
        a_dec = sb("a_dec", [P, T])
        a_mult = sb("a_mult", [P, T])
        q = sb("q", [P, T])
        k = sb("k", [P, T])
        vT = sb("vT", [P, T])
        v_tok = sb("v_tok", [P, TC, P])
        probs = sb("probs", [P, sum(T - j * P for j in range(TC))])
        g_silu = sb("g_silu", [P, T])
        yv = sb("yv", [P, T])
        first_square = [xc, r_gate, i_gate, a_dec, a_mult, q, k, vT]

        gelu_in = [i_gate, a_dec, i_gate, a_dec]
        y_buffer = [tmp1, tmp1, yv, tmp1]
        y_nth = [HEADS - 1, HEADS + 1, HEADS + 2, HEADS + 3]
        y_buffer_reads = [0, HEADS, HEADS + 1, HEADS + 2]

        banks = [ctx.enter_context(nc.psum_tensor(f"out{b}", [P, T], F32)) for b in range(RING)]
        ps_a = ctx.enter_context(nc.psum_tensor("ps_a", [P, T], F32))
        ps_b = ctx.enter_context(nc.psum_tensor("ps_b", [P, T], F32))
        ps_ret = ctx.enter_context(nc.psum_tensor("ps_ret", [P, T], F32))
        ps_sum = ctx.enter_context(nc.psum_tensor("ps_sum", [P, T], F32))
        ps_pair = [ps_a, ps_b]
        scores_in = [(0, ps_a[:, 0:T]), (2, ps_ret[:, 0:2 * P]),
                     (1, ps_b[:, 0:3 * P]), (3, ps_b[:, 3 * P:T])]
        SCORES_BEFORE = {0: 1, 2: 2, 1: 4, 3: 4}

        x_loaded = [sem(f"x_loaded{m}") for m in range(KC)]
        par_loaded = sem("par_loaded")
        pos_loaded = sem("pos_loaded")
        eye_loaded = sem("eye_loaded")
        mix_loaded = sem("mix_loaded")
        w_loaded = [sem(f"w_loaded{s}") for s in range(RING)]
        out_stored = sem("out_stored")
        w_hi_done = sem("w_hi_done")
        w_split = sem("w_split")
        piece_used = sem("piece_used")
        out_read = sem("out_read")
        consts = sem("consts")
        soft_step = sem("soft_step")
        soft_exp = sem("soft_exp")
        angle_step = sem("angle_step")
        trig_step = sem("trig_step")
        trig_done = sem("trig_done")
        xg_hi_done = sem("xg_hi_done")
        xg_ready = sem("xg_ready")
        sq_done = sem("sq_done")
        sum_hi_done = sem("sum_hi_done")
        sum_split = sem("sum_split")
        ones_ready = sem("ones_ready")
        head_hi_done = sem("head_hi_done")
        head_split = sem("head_split")
        sumsq_step = sem("sumsq_step")
        sum_done = sem("sum_done")
        root_done = sem("root_done")
        rms_done = sem("rms_done")
        silu_done = sem("silu_done")
        h_done = sem("h_done")
        h_hi_done = sem("h_hi_done")
        h_ready = sem("h_ready")
        tables_scaled = sem("tables_scaled")
        pad_done = sem("pad_done")
        gate_hi_done = sem("gate_hi_done")
        gate_w_ready = sem("gate_w_ready")
        xc_hi_done = sem("xc_hi_done")
        xc_ready = sem("xc_ready")
        conv0_done = sem("conv0_done")
        conv_step = sem("conv_step")
        gates_done = sem("gates_done")
        sigmoid_done = sem("sigmoid_done")
        decay_step = sem("decay_step")
        ix_done = sem("ix_done")
        mult_sq_done = sem("mult_sq_done")
        mult_done = sem("mult_done")
        u_done = sem("u_done")
        scan_done = sem("scan_done")
        rot_step = sem("rot_step")
        qk_ready = sem("qk_ready")
        scores_done = sem("scores_done")
        probs_ready = sem("probs_ready")
        turned_done = sem("turned_done")
        v_tok_ready = sem("v_tok_ready")
        ret_done = sem("ret_done")
        ret_sq_done = sem("ret_sq_done")
        head_sum_done = sem("head_sum_done")
        head_root_done = sem("head_root_done")
        head_rms_done = sem("head_rms_done")
        ret_read = sem("ret_read")
        y_done = sem("y_done")
        y_hi_done = sem("y_hi_done")
        y_ready = sem("y_ready")
        g_silu_done = sem("g_silu_done")
        gelu_done = sem("gelu_done")
        token_sum_done = sem("token_sum_done")
        token_root_done = sem("token_root_done")
        token_rms_done = sem("token_rms_done")
        diag_done = sem("diag_done")
        spread_done = sem("spread_done")
        last_rms_done = sem("last_rms_done")
        last_xg_done = sem("last_xg_done")
        final_done = sem("final_done")
        final_pool_done = sem("final_pool_done")

        def piece(l, quad, s):
            return l * (LAYER_Q * RING) + quad * RING + s

        def used(n):
            return n + 1 + RING

        def read(o):
            return o + 1 + RING

        def after(count):
            return count + 1

        def norm_index(l, which):
            return l * 3 + which

        def g_col(j, m):
            return par[:, bass.ds(G_AT + j * KC + m, 1)]

        def chan(at, l, c):
            return par[:, bass.ds(at + l * RC + c, 1)]

        def f32(ap):
            return ap.bitcast(F32)

        block = ctx.enter_context(nc.Block())

        X_BEFORE_PIECE = {1: 1, 2: 5, 3: 7}
        X_BY_ACT, X_BY_POOL = (0, 1, 2, 3), (4, 5, 6, 7)

        def load_x(eng, m):
            eng.dma_start(x[:, m, :], xT[m]).then_inc(x_loaded[m], 16)

        BY_POOL = (KC - 2, KC - 1)
        last_xg = {KC - 2: cos, KC - 1: sin}
        diag = tmp0.rearrange("p (c n) -> p c n", c=TC)

        def store(eng, m):
            eng.dma_start(out[m], x[:, m, :]).then_inc(out_stored, 16)

        @block.sync
        def _(sp):
            def load(l, quad, s, blocks, src):
                sp.wait_ge(w_split, piece(l, quad, s) + 1)
                sp.dma_start(raw[:, s, 0:blocks, :].rearrange("p j n -> p (j n)"), src)\
                  .then_inc(w_loaded[s], 16)

            def ffn(l, a):
                with sp.Fori(0, UP_Q) as i:
                    for s in range(RING):
                        if a == 0 and s > 0:
                            sp.wait_ge(x_loaded[X_BEFORE_PIECE[s]], 16)
                        load(l, FFN_AT[a] + i, s, PIECE, w_up[a][l, i, s])
                with sp.Fori(0, DOWN_Q) as m:
                    at = 0
                    for s in range(RING):
                        load(l, FFN_AT[a] + UP_Q + m, s, DOWN[s],
                             w_down[a][l, m, :, at * P:(at + DOWN[s]) * P])
                        at += DOWN[s]

            with sp.Fori(0, DEPTH) as l:
                ffn(l, 0)
                with sp.Fori(0, PROJ_Q) as i:
                    for s in range(RING):
                        load(l, MIX_AT + i, s, PIECE, w_proj[l, i, s])
                with sp.Fori(0, MERGE_Q) as i:
                    for s in range(RING):
                        load(l, MIX_AT + PROJ_Q + i, s, PIECE, w_merge[l, i, s])
                ffn(l, 1)
            for m in range(BY_POOL[0]):
                sp.wait_ge(final_done, m + 1)
                store(sp, m)
            sp.wait_ge(out_stored, 16 * KC)

        @block.gpsimd
        def _(pool):
            pool.memset(one[:], 1.0).then_inc(w_hi_done, 1)
            pool.memset(eps[:], EPS).then_inc(w_split, RING)

            for m in X_BY_POOL:
                load_x(pool, m)

            hi_value = pool.alloc_register("hi_value")

            def split(l, quad, s, blocks):
                n = piece(l, quad, s)
                src = raw[:, s, 0:blocks, :].rearrange("p j n -> p (j n)")
                hi = w_hi[:, s, 0:blocks, :].rearrange("p j n -> p (j n)")
                lo = w_lo[:, s, 0:blocks, :].rearrange("p j n -> p (j n)")
                pool.wait_ge(w_loaded[s], (l * LAYER_Q + quad + 1) * 16)
                pool.wait_ge(piece_used, n + 1)
                pool.reg_add(hi_value, pool.snap(n + 1), 1)
                pool.tensor_scalar(hi, src, 1.0, 0.0, ALU.mult, ALU.add).then_inc(w_hi_done, 1)
                pool.wait_ge(w_hi_done, hi_value)
                pool.tensor_tensor(lo, src, f32(hi), ALU.subtract).then_inc(w_split, 1)

            def phase(l, first_quad, quads, blocks):
                with pool.Fori(0, quads) as i:
                    for s in range(RING):
                        split(l, first_quad + i, s, blocks[s])

            with pool.Fori(0, DEPTH) as l:
                phase(l, FFN_AT[0], UP_Q, [PIECE] * RING)
                phase(l, FFN_AT[0] + UP_Q, DOWN_Q, DOWN)
                phase(l, MIX_AT, MIX_Q, [PIECE] * RING)
                phase(l, FFN_AT[1], UP_Q, [PIECE] * RING)
                phase(l, FFN_AT[1] + UP_Q, DOWN_Q, DOWN)
            pool.wait_ge(last_xg_done, len(BY_POOL))
            pool.wait_ge(last_rms_done, 1)
            for m in BY_POOL:
                pool.tensor_tensor(x[:, m, :], last_xg[m][:], rms[:], ALU.mult)\
                    .then_inc(final_pool_done, 1)

        @block.tensor
        def _(pe):
            pe.sem_inc(piece_used, RING)

            def product(l, quad, s, blocks, rhs_hi, rhs_lo, bank, start, stop, ready=None):
                n = piece(l, quad, s)
                pe.wait_ge(w_split, n + 1 + RING)
                for j, (slot_block, chunk) in enumerate(blocks):
                    if ready:
                        ready(j)
                    hi, lo = w_hi[:, s, slot_block, :], w_lo[:, s, slot_block, :]
                    first, last = start and j == 0, stop and j == len(blocks) - 1
                    pe.matmul(bank[:], hi, rhs_hi[:, chunk, :], start=first, stop=False)
                    pe.matmul(bank[:], hi, rhs_lo[:, chunk, :], start=False, stop=False)
                    mm = pe.matmul(bank[:], lo, rhs_hi[:, chunk, :], start=False, stop=last)
                mm.then_inc(piece_used, 1)

            all_chunks = [(j, j) for j in range(KC)]

            def x_product(l, quad, s, o, ready=None):
                pe.wait_ge(out_read, o + 1)
                product(l, quad, s, all_chunks, xg_hi, xg_lo, banks[s], True, True, ready)

            def partition_sum(split, nth, done):
                pe.wait_ge(split, nth + 1)
                pe.matmul(ps_sum[:], ones[:], sum_hi[:], start=True, stop=False)
                pe.matmul(ps_sum[:], ones[:], sum_lo[:], start=False, stop=True).then_inc(done, 1)

            def sum_squares(j):
                partition_sum(sum_split, j, sum_done)

            def first_quad(l, quad, o, j):
                def chunk_ready(kc):
                    pe.wait_ge(xg_ready, KC * j + kc + 1)
                x_product(l, quad, 0, o, chunk_ready)
                x_product(l, quad, 1, o + 1)
                sum_squares(j)
                for s in range(2, RING):
                    x_product(l, quad, s, o + s)

            def ffn(l, a):
                quad, o, j = FFN_AT[a], l * LAYER_O + FFN_O_AT[a], norm_index(l, NORM_OF_FFN[a])
                first_quad(l, quad, o, j)
                with pe.Fori(1, UP_Q) as i:
                    for s in range(RING):
                        x_product(l, quad + i, s, o + i * RING + s)
                h_base = l * (2 * FC) + a * FC
                with pe.Fori(0, DOWN_Q // RING) as i:
                    for b in range(RING):
                        pe.wait_ge(out_read, o + RING * UP_Q + i * RING + b + 1)
                        at = 0
                        for s in range(RING):
                            def hidden_ready(j, at=at):
                                if at + j == 0:
                                    pe.wait_ge(h_ready, after(h_base + FC - 2))
                                elif at + j >= FC - 2:
                                    pe.wait_ge(h_ready, after(h_base + at + j + 1))
                            product(l, quad + UP_Q + i * RING + b, s,
                                    [(jj, at + jj) for jj in range(DOWN[s])], h_hi, h_lo,
                                    banks[b], s == 0, s == RING - 1, hidden_ready)
                            at += DOWN[s]

            def head_sum(l, h):
                partition_sum(head_split, l * HEADS + h, head_sum_done)

            def head_step(l, h, tail):
                quad, o = MIX_AT + 1 + h, l * LAYER_O + MIX_O_AT + (1 + h) * RING
                x_product(l, quad, 0, o)
                if tail:
                    head_sum(l, h - 1)
                x_product(l, quad, 1, o + 1)
                pe.wait_ge(gate_w_ready, l * RC + h + 1)
                pe.wait_ge(xc_ready, l * RC + h + 1)
                for n in range(2):
                    gate = ps_pair[n]
                    pe.matmul(gate[:], gate_hi[:, n, :], xc_hi[:], start=True, stop=False)
                    pe.matmul(gate[:], gate_hi[:, n, :], xc_lo[:], start=False, stop=False)
                    pe.matmul(gate[:], gate_lo[:, n, :], xc_hi[:], start=False, stop=True)\
                      .then_inc(gates_done, 1)
                x_product(l, quad, 2, o + 2)
                pe.wait_ge(qk_ready, after((l * HEADS + h) * 2 + 2))
                pe.wait_ge(sigmoid_done, (l * RC + h) * 2 + 2)
                pe.wait_ge(ret_read, after(l * HEADS + h))
                for j, place in scores_in:
                    pe.matmul(place, k[:, j * P:(j + 1) * P],
                              q[:, j * P:T], start=True, stop=True).then_inc(scores_done, 1)
                pe.wait_ge(out_read, read(o + 2))
                pe.wait_ge(eye_loaded, 16)
                if tail:
                    pe.wait_ge(head_root_done, l * HEADS + h)
                for j in range(TC):
                    tr = pe.transpose(ps_sum[:, j * P:(j + 1) * P], vT[:, j * P:(j + 1) * P], ident[:])
                tr.then_inc(turned_done, 1)
                x_product(l, quad, 3, o + 3)
                pe.wait_ge(v_tok_ready, l * HEADS + h + 1)
                pe.wait_ge(probs_ready, (l * HEADS + h) * TC + TC)
                at = 0
                for j in range(TC):
                    mm = pe.matmul(ps_ret[:, j * P:T], v_tok[:, j, :], probs[:, at:at + T - j * P],
                                   start=j == 0, stop=j == TC - 1)
                    at += T - j * P
                mm.then_inc(ret_done, 1)

            def mix(l):
                quad, o = MIX_AT, l * LAYER_O + MIX_O_AT
                first_quad(l, quad, o, norm_index(l, NORM_OF_MIX))
                head_step(l, 0, False)
                with pe.Fori(1, HEADS) as h:
                    head_step(l, h, True)
                x_product(l, quad + PROJ_Q - 1, 0, o + RING * (PROJ_Q - 1))
                head_sum(l, HEADS - 1)
                for s in range(1, RING):
                    x_product(l, quad + PROJ_Q - 1, s, o + RING * (PROJ_Q - 1) + s)
                order = [RC, RC + 1, RC + 2, 0, RC + 3, 1, 2, 3]
                with pe.Fori(0, MERGE_Q) as i:
                    for s in range(RING):
                        pe.wait_ge(out_read, o + RING * (PROJ_Q + i) + s + 1)
                        def y_chunk_ready(j):
                            if j == 0 or j >= 3:
                                pe.wait_ge(y_ready, after(l * YS + max(j + 1, 3)))
                        product(l, quad + PROJ_Q + i, s, [(c, c) for c in order], y_hi, y_lo,
                                banks[s], True, True, y_chunk_ready)

            def keep_warm(products):
                for _ in range(products):
                    pe.matmul(ps_ret[:], tmp1[:, 0:P], tmp1[:], start=True, stop=True)

            pe.wait_ge(out_read, RING)
            keep_warm(WARM_UP)
            pe.wait_ge(ones_ready, 1)
            with pe.Fori(0, DEPTH) as l:
                ffn(l, 0)
                mix(l)
                ffn(l, 1)
            keep_warm(WARM_SUM)
            pe.wait_ge(sumsq_step, (KC + 1) * NORMS)
            for c in range(TC):
                mm = pe.matmul(ps_b[:, c:c + 1], sumsq[:, c * P:(c + 1) * P], one[:],
                               start=True, stop=True)
            mm.then_inc(token_sum_done, 1)
            keep_warm(WARM_SPREAD)
            pe.wait_ge(diag_done, TC)
            for bank in (ps_sum, ps_a):
                pe.matmul(bank[:], f32(ones[:]), tmp0[:], start=True, stop=True)\
                  .then_inc(spread_done, 1)

        @block.scalar
        def _(act):
            act.dma_start(par[:], params).then_inc(par_loaded, 16)
            for m in X_BY_ACT:
                load_x(act, m)

            def xg_high(j, m):
                act.activation(xg_hi[:, m, :], x[:, m, :], ACT.Identity, scale=g_col(j, m))\
                   .then_inc(xg_hi_done, 1)

            def x_updates(j, o):
                with act.Fori(0, KC) as m:
                    act.wait_ge(out_read, read(o + m))
                    act.wait_ge(sumsq_step, (KC + 1) * j + m + 1)
                    act.activation(square[:], x[:, m, :], ACT.Square).then_inc(sq_done, 1)
                    xg_high(j, m)
                sum_high(j)

            def sum_high(j):
                act.wait_ge(sumsq_step, (KC + 1) * (j + 1))
                act.activation(sum_hi[:], sumsq[:], ACT.Copy).then_inc(sum_hi_done, 1)

            def root(j):
                act.wait_ge(sum_done, j + 1)
                act.activation(square[:], ps_sum[:], ACT.Sqrt, scale=1.0 / D, bias=eps[:])\
                   .then_inc(root_done, 1)

            def up(l, a):
                root(norm_index(l, NORM_OF_FFN[a]))
                base = l * (2 * FC) + a * FC
                o = l * LAYER_O + FFN_O_AT[a]
                with act.Fori(0, FC) as f:
                    act.wait_ge(out_read, read(o + 2 * f))
                    act.activation(tmp0[:], tmp0[:], ACT.Silu).then_inc(silu_done, 1)
                    act.wait_ge(h_done, base + f + 1)
                    act.activation(h_hi[:, f, :], tmp1[:], ACT.Copy).then_inc(h_hi_done, 1)

            def trig(l):
                act.wait_ge(trig_step, l * TRIG_STEPS + TRIG_STEPS)
                act.activation(sin[0:64, :], cos[0:64, :], ACT.Sin).then_inc(trig_done, 1)
                act.activation(sin[64:P, :], cos[64:P, :], ACT.Sin, scale=-1.0).then_inc(trig_done, 1)
                act.wait_ge(trig_done, 3 * l + 2)
                act.activation(cos[:], tmp1[:], ACT.Sin, scale=-1.0, bias=half_pi[:])\
                   .then_inc(trig_done, 1)

            def head_square(l, h):
                act.wait_ge(ret_done, l * HEADS + h + 1)
                act.activation(square[:], ps_ret[:], ACT.Square).then_inc(ret_sq_done, 1)
                act.wait_ge(ret_sq_done, l * HEADS + h + 1)
                act.activation(sum_hi[:], square[:], ACT.Copy).then_inc(head_hi_done, 1)

            def head_root(l, h):
                act.wait_ge(head_sum_done, l * HEADS + h + 1)
                act.activation(square[:], ps_sum[:], ACT.Sqrt, scale=1.0 / DH, bias=eps[:])\
                   .then_inc(head_root_done, 1)

            def y_high(l, nth, chunk, y=yv):
                act.wait_ge(y_done, l * YS + nth + 1)
                act.activation(y_hi[:, chunk, :], y[:], ACT.Copy).then_inc(y_hi_done, 1)

            def head_step(l, h, tail):
                if tail:
                    head_square(l, h - 1)
                act.wait_ge(out_read, read(l * LAYER_O + MIX_O_AT + h))
                act.activation(xc[:], xr[:, h, TAPS - 1:], ACT.Identity,
                               scale=par[:, bass.ds(CONV_W_AT + (l * TAPS + TAPS - 1) * RC + h, 1)],
                               bias=chan(CONV_B_AT, l, h)).then_inc(conv0_done, 1)
                act.wait_ge(conv_step, (l * RC + h) * 3 + 3)
                act.activation(xc_hi[:], xc[:], ACT.Copy).then_inc(xc_hi_done, 1)
                if tail:
                    head_root(l, h - 1)
                act.wait_ge(scan_done, after(l * RC + h))
                act.wait_ge(gates_done, (l * RC + h) * 2 + 1)
                act.activation(r_gate[:], ps_a[:], ACT.Sigmoid, bias=chan(GATE_A_B_AT, l, h))\
                   .then_inc(sigmoid_done, 1)
                act.wait_ge(gates_done, (l * RC + h) * 2 + 2)
                act.activation(i_gate[:], ps_b[:], ACT.Sigmoid, bias=chan(GATE_X_B_AT, l, h))\
                   .then_inc(sigmoid_done, 1)
                if tail:
                    y_high(l, h - 1, RC + h - 1)
                act.wait_ge(sigmoid_done, (l * RC + h) * 2 + 1)
                act.activation(a_dec[:], r_gate[:], ACT.Exp, scale=lru_neg[:, bass.ds(l * RC + h, 1)])\
                   .then_inc(decay_step, 1)
                act.activation(a_mult[:], r_gate[:], ACT.Tanh, scale=lru_pos[:, bass.ds(l * RC + h, 1)])\
                   .then_inc(decay_step, 1)
                act.wait_ge(decay_step, (l * RC + h) * 3 + 2)
                act.activation(r_gate[:], a_dec[:], ACT.Square).then_inc(decay_step, 1)
                act.wait_ge(turned_done, l * HEADS + h + 1)
                act.activation(v_tok[:].rearrange("p j n -> p (j n)"), ps_sum[:], ACT.Copy)\
                   .then_inc(v_tok_ready, 1)
                act.wait_ge(mult_sq_done, l * RC + h + 1)
                act.activation(a_mult[:], a_mult[:], ACT.Sqrt).then_inc(mult_done, 1)
                act.wait_ge(out_read, read(l * LAYER_O + MIX_O_AT + (1 + h) * RING + 3))
                act.activation(g_silu[:], g_silu[:], ACT.Silu).then_inc(g_silu_done, 1)

            def gelu(l, c):
                act.wait_ge(out_read, read(l * LAYER_O + MIX_O_AT + RING * (PROJ_Q - 1) + c))
                act.activation(gelu_in[c][:], gelu_in[c][:], ACT.Gelu_apprx_tanh)\
                   .then_inc(gelu_done, 1)

            def mix(l):
                act.wait_ge(piece_used, used(piece(l, MIX_AT - 1, RING - 1)))
                act.dma_start(dec[:], decay).then_inc(mix_loaded, 16)
                act.dma_start(gate_w[:], gates[l]).then_inc(mix_loaded, 16)
                root(norm_index(l, NORM_OF_MIX))
                head_step(l, 0, False)
                with act.Fori(1, HEADS) as h:
                    head_step(l, h, True)
                head_square(l, HEADS - 1)
                gelu(l, 0)
                y_high(l, HEADS - 1, 0, y_buffer[0])
                head_root(l, HEADS - 1)
                gelu(l, 1)
                y_high(l, HEADS, RC + HEADS - 1)
                y_high(l, HEADS + 1, 1, y_buffer[1])
                for c in range(2, RC):
                    gelu(l, c)
                    y_high(l, HEADS + c, c, y_buffer[c])
                x_updates(norm_index(l, NORM_OF_MIX) + 1, l * LAYER_O + MIX_O_AT + RING * PROJ_Q)

            act.wait_ge(consts, 2)
            act.activation(ones[:], square[:, 0:P], ACT.Copy).then_inc(ones_ready, 1)
            act.wait_ge(soft_step, 1)
            act.activation(soft[:, 1, :], soft[:, 0, :], ACT.Exp, scale=-1.0).then_inc(soft_exp, 1)
            for m in range(KC):
                act.wait_ge(x_loaded[m], 16)
                xg_high(0, m)
            act.dma_start(angle[:].bitcast(I32), positions).then_inc(pos_loaded, 16)
            act.dma_start(ident[:], eye).then_inc(eye_loaded, 16)
            for m in range(KC):
                act.activation(first_square[m][:], x[:, m, :], ACT.Square).then_inc(sq_done, 1)
            sum_high(0)
            with act.Fori(0, DEPTH) as l:
                up(l, 0)
                trig(l)
                x_updates(norm_index(l, NORM_OF_FFN[0]) + 1, l * LAYER_O + FFN_O_AT[0] + RING * UP_Q)
                mix(l)
                up(l, 1)
                x_updates(norm_index(l, NORM_OF_FFN[1]) + 1, l * LAYER_O + FFN_O_AT[1] + RING * UP_Q)
            act.wait_ge(token_sum_done, 1)
            act.activation(token_rms[:], ps_b[:, 0:TC], ACT.Sqrt, scale=1.0 / D, bias=eps[:])\
               .then_inc(token_root_done, 1)
            for m in BY_POOL:
                act.activation(last_xg[m][:], x[:, m, :], ACT.Identity, scale=g_col(NORMS - 1, m))\
                   .then_inc(last_xg_done, 1)
            act.wait_ge(spread_done, 2)
            act.activation(rms[:], ps_a[:], ACT.Copy).then_inc(last_rms_done, 1)
            for nth, m in enumerate(BY_POOL):
                act.wait_ge(final_pool_done, nth + 1)
                store(act, m)

        @block.vector
        def _(dve):
            for credit in (h_ready, qk_ready, scan_done, ret_read, y_ready):
                dve.sem_inc(credit, 1)
            dve.memset(square[:, 0:P], 1.0).then_inc(consts, 1)
            dve.memset(half_pi[:], TWO_PI / 4).then_inc(consts, 1)
            dve.memset(sumsq[:], 0.0).then_inc(sumsq_step, 1)
            dve.memset(tmp1[:], 0.0).then_inc(out_read, RING)

            def clear_sum():
                dve.memset(sumsq[:], 0.0).then_inc(sumsq_step, 1)

            def norm_prep(j, m):
                add_square(j, m, square)
                xg_low(j, m)

            def add_square(j, m, x_squared):
                dve.wait_ge(sq_done, KC * j + m + 1)
                dve.wait_ge(sumsq_step, (KC + 1) * j + m + 1)
                dve.tensor_tensor(sumsq[:], sumsq[:], x_squared[:], ALU.add).then_inc(sumsq_step, 1)

            def xg_low(j, m):
                dve.wait_ge(xg_hi_done, KC * j + m + 1)
                dve.scalar_tensor_tensor(xg_lo[:, m, :], x[:, m, :], g_col(j, m), f32(xg_hi[:, m, :]),
                                         ALU.mult, ALU.subtract).then_inc(xg_ready, 1)

            def sum_low(j):
                dve.wait_ge(sum_hi_done, j + 1)
                dve.tensor_tensor(sum_lo[:], sumsq[:], f32(sum_hi[:]), ALU.subtract)\
                   .then_inc(sum_split, 1)

            def factor(j):
                dve.wait_ge(root_done, j + 1)
                dve.reciprocal(rms[:], square[:]).then_inc(rms_done, 1)

            def residual(l, quad, last_slot, o, j, m, bank, scale):
                dve.wait_ge(piece_used, used(piece(l, quad, last_slot)))
                dve.scalar_tensor_tensor(x[:, m, :], bank[:], scale, x[:, m, :], ALU.mult, ALU.add)\
                   .then_inc(out_read, 1)
                norm_prep(j, m)

            def ffn(l, a):
                quad, o, j = FFN_AT[a], l * LAYER_O + FFN_O_AT[a], norm_index(l, NORM_OF_FFN[a])
                base = l * (2 * FC) + a * FC
                factor(j)
                with dve.Fori(0, UP_Q) as i:
                    for b in range(2):
                        f = i * 2 + b
                        dve.wait_ge(rms_done, j + 1)
                        dve.wait_ge(piece_used, used(piece(l, quad + i, 2 * b)))
                        dve.tensor_tensor(tmp0[:], banks[2 * b][:], rms[:], ALU.mult)\
                           .then_inc(out_read, 1)
                        dve.wait_ge(h_ready, after(base + f))
                        dve.wait_ge(piece_used, used(piece(l, quad + i, 2 * b + 1)))
                        dve.tensor_tensor(tmp1[:], banks[2 * b + 1][:], rms[:], ALU.mult)\
                           .then_inc(out_read, 1)
                        dve.wait_ge(silu_done, base + f + 1)
                        dve.wait_ge(out_read, read(o + i * RING + 2 * b + 1))
                        dve.tensor_tensor(tmp1[:], tmp0[:], tmp1[:], ALU.mult).then_inc(h_done, 1)
                        dve.wait_ge(h_hi_done, base + f + 1)
                        dve.wait_ge(h_done, base + f + 1)
                        dve.tensor_tensor(h_lo[:, f, :], tmp1[:], f32(h_hi[:, f, :]), ALU.subtract)\
                           .then_inc(h_ready, 1)
                clear_sum()
                if a == 0:
                    trig(l)
                with dve.Fori(0, DOWN_Q // RING) as i:
                    for b in range(RING):
                        residual(l, quad + UP_Q + i * RING + b, RING - 1,
                                 o + RING * UP_Q + i * RING + b, j + 1, i * RING + b, banks[b], 0.5)
                sum_low(j + 1)

            def trig(l):
                n, n_hi, y = tmp0, tmp1, cos
                step = [0]

                def did(ins):
                    ins.then_inc(trig_step, 1)
                    step[0] += 1
                    if step[0] < TRIG_STEPS:
                        dve.wait_ge(trig_step, l * TRIG_STEPS + step[0])

                dve.wait_ge(h_ready, after(l * (2 * FC) + FC))
                did(dve.tensor_scalar(n[:], angle[:], 1 / TWO_PI, ROUND, ALU.mult, ALU.add))
                did(dve.tensor_scalar(n[:], n[:], -ROUND, None, ALU.add))
                did(dve.tensor_scalar(n_hi[:], n[:], 1 / TURN, ROUND, ALU.mult, ALU.add))
                did(dve.tensor_scalar(n_hi[:], n_hi[:], -ROUND, None, ALU.add))
                did(dve.scalar_tensor_tensor(n[:], n_hi[:], -TURN, n[:], ALU.mult, ALU.add))
                src = angle
                for part in TURN_PARTS:
                    for count, size in ((n_hi, TURN), (n, 1.0)):
                        did(dve.scalar_tensor_tensor(y[:], count[:], -part * size, src[:],
                                                     ALU.mult, ALU.add))
                        src = y
                did(dve.tensor_scalar(n[:], y[:], 1 / TWO_PI, ROUND, ALU.mult, ALU.add))
                did(dve.tensor_scalar(n[:], n[:], -ROUND, None, ALU.add))
                did(dve.scalar_tensor_tensor(y[:], n[:], -TWO_PI, y[:], ALU.mult, ALU.add))
                did(dve.tensor_scalar(y[:], y[:], PI_BELOW, -PI_BELOW, ALU.min, ALU.max))
                did(dve.scalar_tensor_tensor(n_hi[:], y[:], -1.0, y[:], ALU.mult, ALU.max))
                assert step[0] == TRIG_STEPS

            def rotary(l, h, which, quad, o, dst):
                bank = banks[which]
                nth = (l * HEADS + h) * 2 + which
                dve.wait_ge(qk_ready, after(nth))
                dve.wait_ge(piece_used, used(piece(l, quad, which)))
                dve.tensor_tensor(tmp0[:], bank[:], cos[:], ALU.mult).then_inc(rot_step, 1)
                dve.tensor_tensor(tmp1[0:64, :], bank[64:P, :], sin[64:P, :], ALU.mult)\
                   .then_inc(rot_step, 1)
                dve.tensor_tensor(tmp1[64:P, :], bank[0:64, :], sin[0:64, :], ALU.mult)\
                   .then_inc(out_read, 1)
                dve.wait_ge(rot_step, nth * 2 + 2)
                dve.wait_ge(out_read, read(o + which))
                dve.tensor_tensor(dst[:], tmp0[:], tmp1[:], ALU.add).then_inc(qk_ready, 1)

            def y_low(l, nth, chunk, y=yv):
                dve.wait_ge(y_hi_done, l * YS + nth + 1)
                dve.tensor_tensor(y_lo[:, chunk, :], y[:], f32(y_hi[:, chunk, :]), ALU.subtract)\
                   .then_inc(y_ready, 1)

            def head_factor(l, h):
                dve.wait_ge(head_root_done, l * HEADS + h + 1)
                dve.reciprocal(square[:], square[:]).then_inc(head_rms_done, 1)

            def head_scaled(l, h, yv_reads):
                dve.wait_ge(head_rms_done, l * HEADS + h + 1)
                dve.wait_ge(y_ready, after(yv_reads))
                dve.tensor_tensor(yv[:], ps_ret[:], square[:], ALU.mult).then_inc(ret_read, 1)

            def head_out(l, h):
                dve.wait_ge(ret_read, after(l * HEADS + h + 1))
                dve.wait_ge(g_silu_done, l * HEADS + h + 1)
                dve.tensor_tensor(yv[:], yv[:], g_silu[:], ALU.mult).then_inc(y_done, 1)

            def head_low(l, h):
                dve.wait_ge(head_hi_done, l * HEADS + h + 1)
                dve.tensor_tensor(sum_lo[:], square[:], f32(sum_hi[:]), ALU.subtract)\
                   .then_inc(head_split, 1)

            def head_step(l, h, tail):
                quad, o = MIX_AT + 1 + h, l * LAYER_O + MIX_O_AT + (1 + h) * RING
                if tail:
                    head_low(l, h - 1)
                dve.tensor_copy(gate_hi[:], gate_w[:, :, h, :]).then_inc(gate_hi_done, 1)
                dve.wait_ge(conv0_done, l * RC + h + 1)
                for t in range(TAPS - 1):
                    if t:
                        dve.wait_ge(conv_step, (l * RC + h) * 3 + t)
                    dve.scalar_tensor_tensor(
                        xc[:], xr[:, h, t:t + T],
                        par[:, bass.ds(CONV_W_AT + (l * TAPS + t) * RC + h, 1)], xc[:],
                        ALU.mult, ALU.add).then_inc(conv_step, 1)
                dve.wait_ge(gate_hi_done, l * RC + h + 1)
                dve.tensor_tensor(gate_lo[:], gate_w[:, :, h, :], f32(gate_hi[:]), ALU.subtract)\
                   .then_inc(gate_w_ready, 1)
                rotary(l, h, 0, quad, o, q)
                dve.wait_ge(xc_hi_done, l * RC + h + 1)
                dve.tensor_tensor(xc_lo[:], xc[:], f32(xc_hi[:]), ALU.subtract).then_inc(xc_ready, 1)
                if tail:
                    head_factor(l, h - 1)
                    head_scaled(l, h - 1, l * YS + (h - 1))
                rotary(l, h, 1, quad, o, k)
                if tail:
                    head_out(l, h - 1)
                dve.wait_ge(piece_used, used(piece(l, quad, 2)))
                dve.tensor_tensor(vT[:], banks[2][:], rms[:], ALU.mult).then_inc(out_read, 1)
                for j, place in scores_in:
                    at = sum(T - i * P for i in range(j))
                    dve.wait_ge(scores_done, (l * HEADS + h) * TC + SCORES_BEFORE[j])
                    dve.tensor_tensor(probs[:, at:at + T - j * P], place,
                                      dec[:, h, 0:T - j * P], ALU.mult).then_inc(probs_ready, 1)
                if tail:
                    y_low(l, h - 1, RC + h - 1)
                dve.wait_ge(sigmoid_done, (l * RC + h) * 2 + 2)
                dve.tensor_tensor(i_gate[:], i_gate[:], xc[:], ALU.mult).then_inc(ix_done, 1)
                dve.wait_ge(decay_step, (l * RC + h) * 3 + 3)
                dve.scalar_tensor_tensor(a_mult[:], r_gate[:], 1.0, a_mult[:], ALU.add, ALU.mult)\
                   .then_inc(mult_sq_done, 1)
                dve.wait_ge(mult_done, l * RC + h + 1)
                dve.wait_ge(ix_done, l * RC + h + 1)
                dve.tensor_tensor(i_gate[:], i_gate[:], a_mult[:], ALU.mult).then_inc(u_done, 1)
                dve.wait_ge(u_done, l * RC + h + 1)
                dve.tensor_tensor_scan(xr[:, h, 0:T], a_dec[:], i_gate[:], 0.0, ALU.mult, ALU.add)\
                   .then_inc(scan_done, 1)
                dve.wait_ge(piece_used, used(piece(l, quad, 3)))
                dve.tensor_tensor(g_silu[:], banks[3][:], rms[:], ALU.mult).then_inc(out_read, 1)

            def gate_out(l, c):
                dve.wait_ge(piece_used, used(piece(l, MIX_AT + PROJ_Q - 1, c)))
                dve.wait_ge(scan_done, after(l * RC + RC))
                if c >= 2:
                    dve.wait_ge(y_done, l * YS + y_nth[c - 2] + 1)
                dve.tensor_tensor(gelu_in[c][:], banks[c][:], rms[:], ALU.mult).then_inc(out_read, 1)

            def rnn_out(l, c):
                dve.wait_ge(gelu_done, l * RC + c + 1)
                dve.wait_ge(y_ready, after(l * YS + y_buffer_reads[c]))
                dve.tensor_tensor(y_buffer[c][:], gelu_in[c][:], xr[:, c, 0:T], ALU.mult)\
                   .then_inc(y_done, 1)

            def rnn_low(l, c):
                dve.wait_ge(y_done, l * YS + y_nth[c] + 1)
                y_low(l, y_nth[c], c, y_buffer[c])

            def mix(l):
                quad, o, j = MIX_AT, l * LAYER_O + MIX_O_AT, norm_index(l, NORM_OF_MIX)
                factor(j)
                dve.wait_ge(rms_done, j + 1)
                dve.wait_ge(trig_done, 3 * (l + 1))
                dve.tensor_tensor(cos[:], cos[:], rms[:], ALU.mult).then_inc(tables_scaled, 1)
                dve.tensor_tensor(sin[:], sin[:], rms[:], ALU.mult).then_inc(tables_scaled, 1)
                dve.memset(xr[:, :, 0:TAPS - 1], 0.0).then_inc(pad_done, 1)
                for c in range(RC):
                    dve.wait_ge(piece_used, used(piece(l, quad, c)))
                    dve.tensor_tensor(xr[:, c, TAPS - 1:], banks[c][:], rms[:], ALU.mult)\
                       .then_inc(out_read, 1)
                dve.wait_ge(pad_done, l + 1)
                dve.wait_ge(tables_scaled, 2 * (l + 1))
                dve.wait_ge(mix_loaded, 32 * (l + 1))
                head_step(l, 0, False)
                with dve.Fori(1, HEADS) as h:
                    head_step(l, h, True)
                head_low(l, HEADS - 1)
                gate_out(l, 0)
                rnn_out(l, 0)
                rnn_low(l, 0)
                head_factor(l, HEADS - 1)
                gate_out(l, 1)
                head_scaled(l, HEADS - 1, l * YS + HEADS)
                head_out(l, HEADS - 1)
                rnn_out(l, 1)
                y_low(l, HEADS, RC + HEADS - 1)
                rnn_low(l, 1)
                for c in range(2, RC):
                    gate_out(l, c)
                    rnn_out(l, c)
                    rnn_low(l, c)
                clear_sum()
                with dve.Fori(0, MERGE_Q) as i:
                    for b in range(RING):
                        residual(l, quad + PROJ_Q + i, b, o + RING * (PROJ_Q + i) + b,
                                 j + 1, i * RING + b, banks[b], 1.0)
                sum_low(j + 1)

            lam = par[:, LAM_AT:LAM_AT + DEPTH * RC]
            magnitude, expo, series, s2 = (soft[:, i, :] for i in range(4))
            step = [0]

            def did(ins):
                ins.then_inc(soft_step, 1)
                step[0] += 1
                dve.wait_ge(soft_step, step[0])

            dve.wait_ge(par_loaded, 16)
            did(dve.scalar_tensor_tensor(magnitude, lam, -1.0, lam, ALU.mult, ALU.max))
            for m in range(KC):
                xg_low(0, m)
            for m in range(KC):
                add_square(0, m, first_square[m])
            sum_low(0)
            dve.wait_ge(soft_exp, 1)
            did(dve.tensor_scalar(magnitude, expo, 2.0, None, ALU.add))
            did(dve.reciprocal(magnitude, magnitude))
            did(dve.tensor_tensor(expo, expo, magnitude, ALU.mult))
            did(dve.tensor_tensor(s2, expo, expo, ALU.mult))
            did(dve.tensor_scalar(series, s2, 1.0 / 17, None, ALU.mult))
            for odd in (15, 13, 11, 9, 7, 5, 3):
                did(dve.scalar_tensor_tensor(series, series, 1.0 / odd, s2, ALU.add, ALU.mult))
            did(dve.scalar_tensor_tensor(series, series, 1.0, expo, ALU.add, ALU.mult))
            did(dve.tensor_scalar(magnitude, lam, -1.0, 0.0, ALU.mult, ALU.max))
            did(dve.scalar_tensor_tensor(series, series, 2.0, magnitude, ALU.mult, ALU.add))
            did(dve.tensor_scalar(lru_pos[:], series, LRU_C, None, ALU.mult))
            did(dve.tensor_scalar(lru_neg[:], series, -LRU_C, None, ALU.mult))
            dve.wait_ge(pos_loaded, 16)
            dve.tensor_copy(tmp0[:], angle[:].bitcast(I32)).then_inc(angle_step, 1)
            dve.wait_ge(angle_step, 1)
            dve.tensor_scalar(angle[:], tmp0[:], par[:, FREQ_AT:FREQ_AT + 1], None, ALU.mult)\
               .then_inc(angle_step, 1)
            dve.wait_ge(angle_step, 2)

            with dve.Fori(0, DEPTH) as l:
                ffn(l, 0)
                mix(l)
                ffn(l, 1)
            dve.wait_ge(token_root_done, 1)
            dve.reciprocal(token_rms[:], token_rms[:]).then_inc(token_rms_done, 1)
            dve.wait_ge(token_rms_done, 1)
            for c in range(TC):
                dve.tensor_scalar(diag[:, c, :], ident[:], token_rms[:, c:c + 1], None, ALU.mult)\
                   .then_inc(diag_done, 1)
            dve.wait_ge(spread_done, 1)
            for m in range(BY_POOL[0]):
                dve.scalar_tensor_tensor(x[:, m, :], x[:, m, :], g_col(NORMS - 1, m), ps_sum[:],
                                         ALU.mult, ALU.mult).then_inc(final_done, 1)


def kernel(**inputs):
    import numpy as _np
    import concourse.bacc as _bacc
    from concourse import mybir as _mybir
    from concourse.bass_utils import run_bass_kernel_spmd as _run

    a = {name: _np.asarray(value) for name, value in inputs.items()}

    def chunks(v):
        return _np.moveaxis(v.reshape(-1, P), -1, 0)

    def up_pieces(w):
        w = w.reshape(DEPTH, KC, P, 2, FC, P)
        return w.transpose(0, 4, 3, 2, 1, 5).reshape(DEPTH, UP_Q, RING, P, KC * P)

    def down_pieces(w):
        return w.reshape(DEPTH, FC, P, KC, P).transpose(0, 3, 2, 1, 4).reshape(DEPTH, KC, P, FF)

    def proj_pieces(w):
        w = w.reshape(DEPTH, KC, P, 6, RC, P)
        by_chunk = w.transpose(0, 3, 4, 2, 1, 5)
        heads = by_chunk[:, 2:6].transpose(0, 2, 1, 3, 4, 5)
        order = _np.concatenate([by_chunk[:, 0:1], heads, by_chunk[:, 1:2]], axis=1)
        return order.reshape(DEPTH, PROJ_Q, RING, P, KC * P)

    def merge_pieces(w):
        return w.reshape(DEPTH, KC, P, KC, P).transpose(0, 3, 2, 1, 4)\
                .reshape(DEPTH, MERGE_Q, RING, P, KC * P)

    norms = _np.concatenate([_np.stack([a["norm_ffn1"], a["norm_mix"], a["norm_ffn2"]], axis=1)
                             .reshape(-1, D), a["norm_final"].reshape(1, D)])
    freq = (10000.0 ** (-_np.arange(DH // 2) / (DH // 2))).astype(_np.float32)
    params = _np.concatenate([
        chunks(norms), chunks(a["conv_w"]), chunks(a["conv_b"]), chunks(a["gate_a_b"]),
        chunks(a["gate_x_b"]), chunks(a["lru_lambda"]), _np.concatenate([freq, freq])[:, None]],
        axis=1)
    half = P // 2
    gates = _np.zeros((DEPTH, P, 2, RC, P), a["gate_a_w"].dtype)
    for n, name in enumerate(("gate_a_w", "gate_x_w")):
        blocks = a[name].reshape(DEPTH, RC, 2, half, half)
        for b in range(2):
            gates[:, b * half:(b + 1) * half, n, :, b * half:(b + 1) * half] = \
                blocks[:, :, b].transpose(0, 2, 1, 3)
    gamma = 1.0 - 2.0 ** (-5.0 - _np.arange(HEADS))
    rel = _np.arange(T)[None, :] - _np.arange(P)[:, None]
    decay = _np.where(rel[:, None, :] >= 0,
                      gamma[None, :, None] ** _np.maximum(rel, 0)[:, None, :], 0.0) * DH ** -0.5

    arrays = {
        "in_x": a["x"].reshape(T, KC, P).transpose(1, 2, 0),
        "in_positions": _np.repeat(a["positions"].reshape(1, T), P, axis=0),
        "in_params": params,
        "in_up0": up_pieces(a["w_ffn1_in"]),
        "in_up1": up_pieces(a["w_ffn2_in"]),
        "in_down0": down_pieces(a["w_ffn1_out"]),
        "in_down1": down_pieces(a["w_ffn2_out"]),
        "in_proj": proj_pieces(a["w_in"]),
        "in_merge": merge_pieces(a["w_out"]),
        "in_gates": gates,
        "in_decay": decay.astype(_np.float32),
        "in_eye": _np.eye(P, dtype=_np.float32),
    }
    arrays = {name: _np.ascontiguousarray(v) for name, v in arrays.items()}
    nc = _bacc.Bacc("TRN2", target_bir_lowering=False, num_devices=1)
    t = {name: nc.dram_tensor(name, v.shape, _mybir.dt.from_np(v.dtype), kind="ExternalInput").ap()
         for name, v in arrays.items()}
    out = nc.dram_tensor("out_x", (KC, P, T), _mybir.dt.float32, kind="ExternalOutput").ap()
    build(nc, t["in_x"], t["in_positions"], t["in_params"], (t["in_up0"], t["in_up1"]),
          (t["in_down0"], t["in_down1"]), t["in_proj"], t["in_merge"], t["in_gates"],
          t["in_decay"], t["in_eye"], out)
    r = _run(nc, [arrays], core_ids=[0])
    got = r.results[0]["out_x"]
    return _np.ascontiguousarray(got.reshape(D, T).T).reshape(1, T, D)
```
